# Optimizing a Trainium2 kernel written in Bass

```python
import jax
import jax.numpy as jnp
from jax import lax
import numpy as np

D_MODEL = 1024
BATCH = 1
SEQ = 1024
DEPTH = 2

CTX_LEN = 256
GRID_W = 64
HEAD_DIM = 64
GROUP_W = D_MODEL // 4
N_FOURIER_HEADS = GROUP_W // HEAD_DIM
N_Q_HEADS = GROUP_W // HEAD_DIM
N_KV_HEADS = 2
Q_PER_KV = N_Q_HEADS // N_KV_HEADS
KV_W = N_KV_HEADS * HEAD_DIM
WINDOW = 128
ATTN_BLOCK = 128
POOL_WINDOWS = (2, 4, 8, 16)
POOL_CH = GROUP_W // len(POOL_WINDOWS)
N_SGU_HEADS = 4
SGU_HEAD = GROUP_W // N_SGU_HEADS
SGU_CHUNK = 128
N_EXPERT_GROUPS = 4
EXPERTS_PER_GROUP = 8
N_EXPERTS = N_EXPERT_GROUPS * EXPERTS_PER_GROUP
TOP_K_FINE = 2
D_EXPERT = D_MODEL // 2
MOE_BLOCK = 128
ROPE_BASE = 10000.0
LN_EPS = 1e-6
NEG_INF = -1e30
RES_ALPHA = (2 * DEPTH) ** 0.25
INIT_BETA = (8 * DEPTH) ** -0.25

COL_FOURIER = 0
COL_Q = COL_FOURIER + GROUP_W
COL_K = COL_Q + N_Q_HEADS * HEAD_DIM
COL_V = COL_K + KV_W
COL_POOL = COL_V + KV_W
COL_U = COL_POOL + GROUP_W
COL_G = COL_U + GROUP_W
D_IN = COL_G + GROUP_W

kernel_name = 'hybrid_parallel_heads_flow_backbone'

def layer_norm(t, gain=None, bias=None):
    tf = t.astype(jnp.float32)
    mu = tf.mean(-1, keepdims=True)
    var = jnp.square(tf - mu).mean(-1, keepdims=True)
    y = (tf - mu) * lax.rsqrt(var + LN_EPS)
    if gain is not None:
        y = y * gain.astype(jnp.float32) + bias.astype(jnp.float32)
    return y.astype(t.dtype)

def modulate(t, shift, scale):
    return layer_norm(t) * (1 + scale) + shift

def axial_rope_tables(n_tokens):
    rows = n_tokens // GRID_W
    row = jnp.repeat(jnp.arange(rows), GRID_W).astype(jnp.float32)
    col = jnp.tile(jnp.arange(GRID_W), rows).astype(jnp.float32)
    n_freq = HEAD_DIM // 4
    freq = ROPE_BASE ** (-jnp.arange(n_freq, dtype=jnp.float32) / n_freq)
    ang = jnp.stack([row[:, None] * freq, col[:, None] * freq], axis=1)
    return jnp.cos(ang), jnp.sin(ang)

def apply_axial_rope(t, cos, sin):
    b, s, h, d = t.shape
    tf = t.astype(jnp.float32).reshape(b, s, h, 2, 2, d // 4)
    c = cos[None, :, None]
    sn = sin[None, :, None]
    t1, t2 = tf[..., 0, :], tf[..., 1, :]
    out = jnp.stack([t1 * c - t2 * sn, t1 * sn + t2 * c], axis=-2)
    return out.reshape(b, s, h, d).astype(t.dtype)

def to_heads(t, n_heads):
    return t.reshape(t.shape[0], t.shape[1], n_heads, HEAD_DIM)

def split_projection(z):
    return (z[..., COL_FOURIER:COL_Q],
            to_heads(z[..., COL_Q:COL_K], N_Q_HEADS),
            to_heads(z[..., COL_K:COL_V], N_KV_HEADS),
            to_heads(z[..., COL_V:COL_POOL], N_KV_HEADS),
            z[..., COL_POOL:COL_U],
            z[..., COL_U:COL_G],
            z[..., COL_G:D_IN])

def fourier_mix(a, w_fourier):
    b, n, _ = a.shape
    ah = a.astype(jnp.float32).reshape(b, n, N_FOURIER_HEADS, HEAD_DIM)
    f = jnp.fft.fft2(ah, axes=(1, 3), norm='ortho').real
    return f.reshape(b, n, GROUP_W).astype(a.dtype) @ w_fourier

def pool_mix(p, w_pool, pool_scale):
    b, n, _ = p.shape
    pf = p.astype(jnp.float32)
    cs = jnp.pad(jnp.cumsum(pf, axis=1), ((0, 0), (1, 0), (0, 0)))
    pos = jnp.arange(n)
    means = []
    for g, w in enumerate(POOL_WINDOWS):
        lo = jnp.clip(pos - w // 2, 0, n)
        hi = jnp.clip(pos + w // 2, 0, n)
        csg = cs[..., g * POOL_CH:(g + 1) * POOL_CH]
        means.append((csg[:, hi] - csg[:, lo]) / (hi - lo).astype(jnp.float32)[:, None])
    pooled = jnp.stack(means, axis=2) - pf.reshape(b, n, len(POOL_WINDOWS), POOL_CH)
    mixed = jnp.einsum('bngc,gcd->bngd', pooled.astype(p.dtype), w_pool)
    return mixed.reshape(b, n, GROUP_W) * pool_scale

def spatial_gating(u, g, w_sgu, b_sgu):
    b, n, _ = u.shape
    u = jax.nn.gelu(u, approximate=False)
    v = layer_norm(jax.nn.gelu(g, approximate=False))
    vh = v.reshape(b, n // SGU_CHUNK, SGU_CHUNK, N_SGU_HEADS, SGU_HEAD)
    mixed = jnp.einsum('hpq,bcqhd->bcphd', w_sgu, vh) + b_sgu.T[None, None, :, :, None]
    return u * mixed.reshape(b, n, GROUP_W)

def window_attention(q, k, v, kc, vc, sink):
    b, s, _, d = q.shape
    nb = s // ATTN_BLOCK
    n_ctx = kc.shape[1]
    scale = d ** -0.5
    qb = q.reshape(b, nb, ATTN_BLOCK, N_KV_HEADS, Q_PER_KV, d)

    def band(t):
        tp = jnp.pad(t, ((0, 0), (ATTN_BLOCK, ATTN_BLOCK), (0, 0), (0, 0)))
        tp = tp.reshape(b, nb + 2, ATTN_BLOCK, N_KV_HEADS, d)
        return jnp.concatenate([tp[:, :-2], tp[:, 1:-1], tp[:, 2:]], axis=2)

    kw, vw = band(k), band(v)
    s_loc = jnp.einsum('bnikgd,bnjkd->bnkgij', qb, kw).astype(jnp.float32) * scale
    s_ctx = jnp.einsum('bnikgd,bckd->bnkgic', qb, kc).astype(jnp.float32) * scale
    blk = jnp.arange(nb)[:, None, None]
    qpos = blk * ATTN_BLOCK + jnp.arange(ATTN_BLOCK)[None, :, None]
    kpos = (blk - 1) * ATTN_BLOCK + jnp.arange(3 * ATTN_BLOCK)[None, None, :]
    valid = (jnp.abs(qpos - kpos) <= WINDOW) & (kpos >= 0) & (kpos < s)
    s_loc = jnp.where(valid[None, :, None, None], s_loc, NEG_INF)
    sink_l = jnp.broadcast_to(
        sink.astype(jnp.float32).reshape(N_KV_HEADS, Q_PER_KV)[None, None, :, :, None, None],
        s_loc.shape[:-1] + (1,))
    probs = jax.nn.softmax(jnp.concatenate([s_loc, s_ctx, sink_l], axis=-1), axis=-1)
    n_loc = 3 * ATTN_BLOCK
    o = (jnp.einsum('bnkgij,bnjkd->bnikgd', probs[..., :n_loc].astype(v.dtype), vw)
         + jnp.einsum('bnkgic,bckd->bnikgd', probs[..., n_loc:n_loc + n_ctx].astype(vc.dtype), vc))
    return o.reshape(b, s, N_Q_HEADS * d)

def context_attention(qc, kc, vc, sink):
    b, n_ctx, _, d = qc.shape
    qg = qc.reshape(b, n_ctx, N_KV_HEADS, Q_PER_KV, d)
    sc = jnp.einsum('bikgd,bjkd->bkgij', qg, kc).astype(jnp.float32) * (d ** -0.5)
    sink_c = jnp.broadcast_to(
        sink.astype(jnp.float32).reshape(N_KV_HEADS, Q_PER_KV)[None, :, :, None, None],
        sc.shape[:-1] + (1,))
    probs = jax.nn.softmax(jnp.concatenate([sc, sink_c], axis=-1), axis=-1)
    o = jnp.einsum('bkgij,bjkd->bikgd', probs[..., :n_ctx].astype(vc.dtype), vc)
    return o.reshape(b, n_ctx, N_Q_HEADS * d)

def merge_groups(a, y_attn, p, u, g, w_fourier, w_pool, pool_scale, w_sgu, b_sgu, w_out):
    y_four = fourier_mix(a, w_fourier)
    y_pool = pool_mix(p, w_pool, pool_scale)
    y_sgu = spatial_gating(u, g, w_sgu, b_sgu)
    return jnp.concatenate([y_four, y_attn, y_pool, y_sgu], axis=-1) @ w_out

def parallel_mixers(h, hc, w_in, w_fourier, sink, w_pool, pool_scale, w_sgu, b_sgu, w_out,
                    rope_cos, rope_sin, ctx_out):
    a, q, k, v, p, u, g = split_projection(h @ w_in)
    q = apply_axial_rope(q, rope_cos, rope_sin)
    k = apply_axial_rope(k, rope_cos, rope_sin)
    if ctx_out:
        ac, qc, kc, vc, pc, uc, gc = split_projection(hc @ w_in)
    else:
        kvc = hc @ w_in[:, COL_K:COL_POOL]
        kc = to_heads(kvc[..., :KV_W], N_KV_HEADS)
        vc = to_heads(kvc[..., KV_W:], N_KV_HEADS)
    y_attn = window_attention(q, k, v, kc, vc, sink)
    y = merge_groups(a, y_attn, p, u, g, w_fourier, w_pool, pool_scale, w_sgu, b_sgu, w_out)
    if not ctx_out:
        return y, None
    yc_attn = context_attention(qc, kc, vc, sink)
    yc = merge_groups(ac, yc_attn, pc, uc, gc, w_fourier, w_pool, pool_scale, w_sgu, b_sgu, w_out)
    return y, yc

def grouped_experts(t, expert_idx, gates, w_gate, w_up, w_down):
    n_tok, d = t.shape
    k = expert_idx.shape[1]
    n_exp = w_gate.shape[0]
    flat_e = expert_idx.reshape(-1)
    order = jnp.argsort(flat_e)
    se = flat_e[order]
    counts = jnp.bincount(flat_e, length=n_exp)
    padded = (counts + MOE_BLOCK - 1) // MOE_BLOCK * MOE_BLOCK
    pad_end = jnp.cumsum(padded)
    pad_start = pad_end - padded
    start = jnp.cumsum(counts) - counts
    dest = pad_start[se] + jnp.arange(n_tok * k) - start[se]
    n_blocks = -(-(n_tok * k) // MOE_BLOCK) + n_exp
    rows = n_blocks * MOE_BLOCK
    slot_tok = jnp.full((rows,), n_tok, jnp.int32).at[dest].set((order // k).astype(jnp.int32))
    slot_gate = jnp.zeros((rows,), jnp.float32).at[dest].set(gates.reshape(-1)[order])
    block_e = jnp.minimum(jnp.searchsorted(pad_end, jnp.arange(n_blocks) * MOE_BLOCK, side='right'),
                          n_exp - 1)
    t_pad = jnp.concatenate([t, jnp.zeros((1, d), t.dtype)], axis=0)
    xb = t_pad[slot_tok].reshape(n_blocks, MOE_BLOCK, d)

    def expert_block(args):
        xblk, e = args
        hid = jax.nn.silu(xblk @ w_gate[e]) * (xblk @ w_up[e])
        return hid @ w_down[e]

    yb = lax.map(expert_block, (xb, block_e)).reshape(rows, d)
    out = jnp.zeros((n_tok + 1, d), t.dtype).at[slot_tok].add(yb * slot_gate[:, None].astype(yb.dtype))
    return out[:n_tok]

def hier_moe(t, w_router_group, w_router_expert, w_exp_gate, w_exp_up, w_exp_down):
    p_group = jax.nn.softmax((t @ w_router_group).astype(jnp.float32), axis=-1)
    grp = jnp.argmax(p_group, axis=-1).astype(jnp.int32)
    gate_group = jnp.take_along_axis(p_group, grp[:, None], axis=-1)
    logits_e = jnp.einsum('td,dge->tge', t, w_router_expert).astype(jnp.float32)
    logits_sel = jnp.take_along_axis(logits_e, grp[:, None, None], axis=1)[:, 0]
    top_p, top_j = lax.top_k(jax.nn.softmax(logits_sel, axis=-1), TOP_K_FINE)
    top_p = top_p / top_p.sum(-1, keepdims=True)
    expert_idx = grp[:, None] * EXPERTS_PER_GROUP + top_j.astype(jnp.int32)
    return grouped_experts(t, expert_idx, gate_group * top_p, w_exp_gate, w_exp_up, w_exp_down)

def setup_inputs(seed: int = 0) -> dict:
    key = jax.random.key(seed)
    ks = jax.random.split(key, 24)
    f32 = jnp.float32
    L, D = DEPTH, D_MODEL

    def nrm(k, shape, fan_in, gain=1.0):
        return jax.random.normal(k, shape, f32) * (gain * fan_in ** -0.5)

    def std(k, shape, s=1.0):
        return jax.random.normal(k, shape, f32) * s

    return {
        'x': std(ks[0], (BATCH, SEQ, D)),
        'c': std(ks[1], (BATCH, D)),
        'ctx': std(ks[2], (BATCH, CTX_LEN, D)),
        'c_ctx': std(ks[3], (D,)),
        'w_ada': nrm(ks[4], (L, D, 6 * D), D, 0.5),
        'b_ada': std(ks[5], (L, 6 * D), 0.02),
        'w_in': nrm(ks[6], (L, D, D_IN), D),
        'w_fourier': nrm(ks[7], (L, GROUP_W, GROUP_W), GROUP_W),
        'attn_sink': std(ks[8], (L, N_Q_HEADS)),
        'w_pool': nrm(ks[9], (L, len(POOL_WINDOWS), POOL_CH, POOL_CH), POOL_CH),
        'pool_scale': 1.0 + std(ks[10], (L, GROUP_W), 0.1),
        'w_sgu': nrm(ks[11], (L, N_SGU_HEADS, SGU_CHUNK, SGU_CHUNK), SGU_CHUNK),
        'b_sgu': 1.0 + std(ks[12], (L, N_SGU_HEADS, SGU_CHUNK), 0.1),
        'w_out': nrm(ks[13], (L, D, D), D, INIT_BETA),
        'ln1_g': 1.0 + std(ks[14], (L, D), 0.1),
        'ln1_b': std(ks[15], (L, D), 0.02),
        'w_router_group': nrm(ks[16], (L, D, N_EXPERT_GROUPS), D),
        'w_router_expert': nrm(ks[17], (L, D, N_EXPERT_GROUPS, EXPERTS_PER_GROUP), D),
        'w_exp_gate': nrm(ks[18], (L, N_EXPERTS, D, D_EXPERT), D),
        'w_exp_up': nrm(ks[19], (L, N_EXPERTS, D, D_EXPERT), D),
        'w_exp_down': nrm(ks[20], (L, N_EXPERTS, D_EXPERT, D), D_EXPERT, INIT_BETA),
        'ln2_g': 1.0 + std(ks[21], (L, D), 0.1),
        'ln2_b': std(ks[22], (L, D), 0.02),
    }

def reference(x, c, ctx, c_ctx, w_ada, b_ada, w_in, w_fourier, attn_sink, w_pool, pool_scale,
              w_sgu, b_sgu, w_out, ln1_g, ln1_b, w_router_group, w_router_expert,
              w_exp_gate, w_exp_up, w_exp_down, ln2_g, ln2_b):
    b, s, d = x.shape
    rope_cos, rope_sin = axial_rope_tables(s)
    cond_lat = jax.nn.silu(c)
    cond_ctx = jax.nn.silu(c_ctx)
    for layer in range(DEPTH):
        last = layer == DEPTH - 1
        m = (cond_lat @ w_ada[layer] + b_ada[layer])[:, None, :]
        mc = (cond_ctx @ w_ada[layer] + b_ada[layer])[None, None, :]
        sh1, sc1, g1, sh2, sc2, g2 = jnp.split(m, 6, axis=-1)
        csh1, csc1, cg1, csh2, csc2, cg2 = jnp.split(mc, 6, axis=-1)

        h = modulate(x, sh1, sc1)
        hc = modulate(ctx, csh1, csc1)
        y, yc = parallel_mixers(h, hc, w_in[layer], w_fourier[layer], attn_sink[layer], w_pool[layer],
                                pool_scale[layer], w_sgu[layer], b_sgu[layer], w_out[layer],
                                rope_cos, rope_sin, not last)
        x = layer_norm(RES_ALPHA * x + g1 * y, ln1_g[layer], ln1_b[layer])

        h2 = modulate(x, sh2, sc2)
        if last:
            f = hier_moe(h2.reshape(-1, d), w_router_group[layer], w_router_expert[layer],
                         w_exp_gate[layer], w_exp_up[layer], w_exp_down[layer]).reshape(b, s, d)
        else:
            ctx = layer_norm(RES_ALPHA * ctx + cg1 * yc, ln1_g[layer], ln1_b[layer])
            hc2 = modulate(ctx, csh2, csc2)
            tokens = jnp.concatenate([h2.reshape(-1, d), hc2.reshape(-1, d)], axis=0)
            f_all = hier_moe(tokens, w_router_group[layer], w_router_expert[layer],
                             w_exp_gate[layer], w_exp_up[layer], w_exp_down[layer])
            f = f_all[:b * s].reshape(b, s, d)
            fc = f_all[b * s:].reshape(ctx.shape)
            ctx = layer_norm(RES_ALPHA * ctx + cg2 * fc, ln2_g[layer], ln2_b[layer])
        x = layer_norm(RES_ALPHA * x + g2 * f, ln2_g[layer], ln2_b[layer])
    return x


_drawn_inputs = setup_inputs


def setup_inputs(seed=0):
    import zlib

    import numpy as np

    out = dict(_drawn_inputs(seed))
    spreads = {}
    factors = {'ctx': 8.0,
     'c_ctx': 4.513,
     'b_ada': 5.105,
     'attn_sink': 52.038,
     'pool_scale': 7.255,
     'b_sgu': 8.0}
    for name, (base, spread) in spreads.items():
        noise = np.random.default_rng([zlib.crc32(name.encode()), seed]).standard_normal(out[name].shape)
        drawn = base * np.exp(spread * noise) if base else spread * noise
        out[name] = jnp.asarray(drawn.astype(out[name].dtype))
    for name, factor in factors.items():
        out[name] = (out[name] * factor).astype(out[name].dtype)
    return out
```

```python
from contextlib import ExitStack

import numpy as np

import concourse.bass as bass
from concourse import mybir

F32 = mybir.dt.float32
I32 = mybir.dt.int32
ALU = mybir.AluOpType
ACT = mybir.ActivationFunctionType
AX = mybir.AxisListType.X

P = 128
D = 1024
KT = D // P
DEPTH = 2
LAYERS = DEPTH
SEQ, CTX = 1024, 256
LT, CT = SEQ // P, CTX // P
NT = LT + CT
HD = 64
NH, NKV = 4, 2
GW = D // 4
C_F, C_Q, C_K, C_V, C_P, C_U = 0, 256, 512, 640, 768, 1024
D_IN = 1536
DE = D // 2
JT = DE // P
NG, EPG = 4, 8
NE = NG * EPG
NR = NG + NE
FEWEST = LT * 2
NSLOTMAX = (NT * P * 2) // P + NE
NBT = (NSLOTMAX + 4 + 7) // 8 * 8
SCALE = float(HD) ** -0.5
ALPHA = float((2 * DEPTH) ** 0.25)
EPS = 1e-6
NEG = -1e30
PAD = 8
PL = PAD + SEQ + PAD
PW = PL + PAD + CTX + PAD

K_ID, K_TRI, K_ONE, K_ROT, K_CD, K_SD = (i * P for i in range(6))
K_MASK = 6 * P
K_EDGE = K_MASK + 3 * 2 * P
K_IW = K_EDGE + 2 * 16
K_GW = K_IW + 2
K_EW = K_GW + NG
K_IOTA = K_EW + EPG
K_NH = K_IOTA + NBT
K_EPS = K_NH + 1
K_KV = K_EPS + 1
K_N = K_KV + NKV


def constant_tables():
    k = np.zeros((P, K_N))
    r = np.arange(P)
    k[:, K_ID:K_ID + P] = np.eye(P)
    k[:, K_TRI:K_TRI + P] = r[:, None] < r[None, :]
    k[:, K_ONE:K_ONE + P] = 1
    for m in range(P):
        if m % 32 < 16:
            k[m + 16, K_ROT + m] = -1
        else:
            k[m - 16, K_ROT + m] = 1
    ang = 2 * np.pi * np.outer(np.arange(HD), np.arange(HD)) / HD
    for b in range(2):
        s = slice(b * HD, b * HD + HD)
        k[s, K_CD + b * HD:K_CD + b * HD + HD] = np.cos(ang)
        k[s, K_SD + b * HD:K_SD + b * HD + HD] = np.sin(ang)
    full = np.full((P, P), NEG)
    before = np.where(r[None, :] >= r[:, None], 0, NEG)
    after = np.where(r[None, :] <= r[:, None], 0, NEG)
    masks = [(full, after), (before, after), (before, full)]
    k[:, K_MASK:K_EDGE] = np.concatenate([np.concatenate(m, 1) for m in masks], 1)
    for g, w in enumerate((2, 4, 8, 16)):
        p, t, n = slice(g % 2 * HD, g % 2 * HD + HD), g // 2, SEQ
        pos = np.concatenate([np.arange(8), np.arange(n - 8, n)])
        k[p, K_EDGE + 16 * t:K_EDGE + 16 * t + 16] = 1 / (np.minimum(pos + w // 2, n) - np.maximum(pos - w // 2, 0))
        k[p, K_IW + t] = 1 / w
    k[:, K_GW:K_GW + NG] = NG - np.arange(NG)
    k[:, K_EW:K_EW + EPG] = EPG - np.arange(EPG)
    k[:, K_IOTA:K_IOTA + NBT] = np.arange(NBT)
    k[:, K_NH] = -0.5
    k[:, K_EPS] = EPS
    for h in range(NKV):
        k[h * HD:(h + 1) * HD, K_KV + h] = 1
    tok, freq = np.arange(SEQ), 10000.0 ** (-np.arange(16) / 16)
    rope = np.zeros((P, 2, SEQ))
    for m in range(P):
        place = (tok // HD if m % HD < 32 else tok % HD).astype(float)
        a = place * freq[m % 16]
        rope[m, 0], rope[m, 1] = np.cos(a), np.sin(a)

    def dft(n):
        R = n // P
        t = np.zeros((P, R, 4 * P))
        for k1 in range(R):
            a = 2 * np.pi * (np.outer(np.arange(P), k1 + R * np.arange(P)) % n) / n
            c, s = np.cos(a) / np.sqrt(n * HD), np.sin(a) / np.sqrt(n * HD)
            f = -1 if k1 > R // 2 else 1
            t[:, k1] = np.concatenate([c, -s, f * s, f * c], 1)
        return t

    ids = (np.arange(NT)[None, :] * P + r[:, None]).astype(np.int32)
    f = np.float32
    return k.astype(f), rope.astype(f), dft(SEQ).astype(f), dft(CTX)[:, :, :2 * P].astype(f).copy(), ids


class Steps:

    def __init__(self, sem):
        self.sem, self.n, self.base = sem, 0, 0

    def up(self):
        self.n += 1
        return 1

    def at(self):
        return self.base + self.n

    def enter(self, i, per):
        self.base, self.start, self.per = i * per, self.n, per

    def leave(self, times):
        assert self.n - self.start == self.per, (self.n - self.start, self.per)
        self.base, self.n = 0, self.start + times * self.per


def loop(nc, eng, start, end):
    return nc.Fori(start, end, 1, engines=bass.OrderedEngineSet([eng.engine]), hint_back_edge=True)


def over(ap, n):
    return ap.unsqueeze(ap.ndim).to_broadcast(list(ap.shape) + [n])


def across(ap, n):
    return ap.unsqueeze(1).to_broadcast([ap.shape[0], n] + list(ap.shape[1:]))


class Core:
    pass


def at_tile(t, width=P, base=0):
    return bass.ds(t * width + base, width) if not isinstance(t, int) else slice(base + t * width, base + (t + 1) * width)


def semaphores(nc, ctx, suffix):
    taken = []

    def give_back():
        nc.clear_and_free_semaphores(taken)
        nc.all_engine_barrier()
    ctx.callback(give_back)

    def sem(name):
        taken.append(nc.alloc_semaphore(name + suffix))
        return taken[-1]
    return sem


class Norm:

    def __init__(self, sb, sem, name, width):
        self.w = min(width, 512)
        self.stats, self.mv, self.rstd = sb(name + "_stats", [P, width // self.w, 6]), sb(name + "_mv", [P, 2]), sb(name + "_rstd", [P, 1])
        self.spare = sb(name + "_spare", [P, 1])
        self.var_ready, self.eps_added, self.rstd_ready = (
            sem(f"{name}_{what}") for what in ("var_ready", "eps_added", "rstd_ready"))


def norm_power(nc, pool, g, r, n):
    pool.wait_ge(r.var_ready, n + 1)
    nc.gpsimd.tensor_tensor(r.rstd[:, :], r.mv[:, 1:2], g.k[:, K_EPS:K_EPS + 1], ALU.add).then_inc(r.eps_added, 1)
    pool.wait_ge(r.eps_added, n + 1)
    nc.gpsimd.tensor_tensor(r.rstd[:, :], r.rstd[:, :], g.k[:, K_NH:K_NH + 1], ALU.pow).then_inc(r.rstd_ready, 1)


def rows_norm(nc, v, s, src, dst, r, n):
    nc.vector.memset(r.spare[:, :], 0.0)
    for j in range(src.shape[-1] // r.w):
        nc.vector.bn_stats(r.stats[:, j, :], src[:, j * r.w:(j + 1) * r.w]).then_inc(s.sem, s.up())
    v.wait_ge(s.sem, s.at())
    nc.vector.memset(r.spare[:, :], 0.0)
    nc.vector.bn_aggr(r.mv[:, :], r.stats[:, :, :].rearrange("p a b -> p (a b)")).then_inc(r.var_ready, 1)
    v.wait_ge(r.rstd_ready, n + 1)
    return nc.vector.tensor_scalar(dst, src, r.mv[:, 0:1], r.rstd[:, :], ALU.subtract, ALU.mult)


def modulation(nc, g):
    a = g.a
    NC = 6 * D // 512
    with ExitStack() as ctx:
        sb = lambda n, s, dt=F32: ctx.enter_context(nc.sbuf_tensor(n, s, dt))
        sem = semaphores(nc, ctx, "")
        NW = 4
        w = [sb(f"ada_w{i}", [P, KT, 512]) for i in range(NW)]
        cond = sb("cond", [P, 2, KT])
        act_c = sb("cond_silu", [P, KT, 2])
        row = sb("ada_row", [2, DEPTH, 6 * D])
        ps = [ctx.enter_context(nc.psum_tensor(f"ada_ps{i}", [P, 512], F32)) for i in range(NW)]
        c_in, k_in, x_in, b_in = sem("c_in"), sem("consts_in"), sem("x_in"), sem("bias_in")
        w_in = [sem(f"ada_w_in{i}") for i in range(NW)]
        w_used, silu_done, ps_free = sem("ada_w_used"), sem("silu_done"), sem("ada_ps_free")
        stored, cols_in, scaled = sem("mods_stored"), sem("cols_in"), sem("cols_scaled")
        CHUNKS = DEPTH * NC

        with nc.Block() as block:
            @block.sync
            def _(sp):
                sp.dma_start(cond[:, 0, :], a["c"].rearrange("a (p k) -> p (a k)", k=KT)).then_inc(c_in, 16)
                sp.dma_start(cond[:, 1, :], a["c_ctx"].rearrange("(p k) -> p k", k=KT)).then_inc(c_in, 16)
                for s in range(2):
                    sp.dma_start(row[s:s + 1, :, :], a["b_ada"].rearrange("(a l) n -> a l n", a=1)).then_inc(b_in, 16)
                for l in range(DEPTH):
                    wl = a["w_ada"][l].rearrange("(p k) n -> p k n", k=KT)
                    with loop(nc, sp, 0, NC // NW) as i:
                        for c in range(NW):
                            sp.wait_ge(w_used, i * NW + l * NC + c + 1)
                            sp.dma_start(w[c][:, :, :], wl[:, :, bass.ds(i * (NW * 512) + c * 512, 512)]).then_inc(w_in[c], 16)
                sp.dma_start(g.k[:, :], a["consts"]).then_inc(k_in, 16)
                sp.dma_start(g.ids[:, :], a["token_ids"]).then_inc(k_in, 16)
                sp.dma_start(g.x[:, 0:LT, :], a["x"][0].rearrange("(t p) d -> p t d", p=P)).then_inc(x_in, 16)
                sp.dma_start(g.x[:, LT:NT, :], a["ctx"][0].rearrange("(t p) d -> p t d", p=P)).then_inc(x_in, 16)
                sp.wait_ge(k_in, 32)
                sp.wait_ge(x_in, 32)

            @block.scalar
            def _(act):
                act.wait_ge(c_in, 32)
                nc.scalar.activation(act_c[:, :, :].rearrange("p k s -> p s k"), cond[:, :, :], ACT.Silu).then_inc(silu_done, 1)
                for l in range(DEPTH):
                    act.wait_ge(ps_free, NW + NC * (l + 1))
                    act.dma_start(g.mods[l], row[:, l, :]).then_inc(stored, 16)
                    act.wait_ge(stored, 16 * (l + 1))
                    for s in range(2):
                        for h in range(2):
                            act.dma_start(g.cols[:, l, s, h, :],
                                          g.mods[l, s, h * D:(h + 1) * D].rearrange("(p k) -> p k", k=KT)).then_inc(cols_in, 16)

            @block.tensor
            def _(pe):
                pe.nop().then_inc(w_used, NW)
                pe.wait_ge(silu_done, 1)
                with loop(nc, pe, 0, CHUNKS // NW) as i:
                    for c in range(NW):
                        pe.wait_ge(w_in[c], i * 16 + 16)
                        pe.wait_ge(ps_free, i * NW + c + 1)
                        for k in range(KT):
                            for j in range(4):
                                mm = nc.tensor.matmul(ps[c][32 * j:32 * j + 2, 0:P], act_c[:, k, :],
                                                      w[c][:, k, j * P:(j + 1) * P], start=k == 0, stop=k == KT - 1)
                        mm.then_inc(w_used, 1)

            @block.vector
            def _(v):
                nc.vector.engine_nop().then_inc(ps_free, NW)
                v.wait_ge(b_in, 32)
                for l in range(DEPTH):
                    with loop(nc, v, 0, NC // NW) as i:
                        for c in range(NW):
                            v.wait_ge(w_used, i * NW + NC * l + c + 1 + NW)
                            for j in range(4):
                                n = row[:, l, bass.ds(i * (NW * 512) + c * 512 + j * P, P)]
                                add = nc.vector.tensor_tensor(n, ps[c][32 * j:32 * j + 2, 0:P], n, ALU.add)
                            add.then_inc(ps_free, 1)
                v.wait_ge(cols_in, 16 * 8)
                nc.vector.tensor_scalar(g.cols[:, :, :, 1, :], g.cols[:, :, :, 1, :], 1.0, None, ALU.add).then_inc(scaled, 1)
                v.wait_ge(scaled, 1)


def combine(nc, v, s, g, t, ya, yb, g2, lng, lnb, r, used, dst):
    x = g.x[:, bass.ds(t, 1), :].rearrange("p a d -> p (a d)")
    gate = g.gate[:, bass.ds(t, 1), :].rearrange("p a d -> p (a d)")
    nc.vector.tensor_scalar(ya, ya, gate[:, 0:1], None, ALU.mult).then_inc(s.sem, s.up())
    v.wait_ge(s.sem, s.at())
    nc.vector.scalar_tensor_tensor(ya, yb, gate[:, 1:2], ya, ALU.mult, ALU.add).then_inc(used, 1)
    v.wait_ge(used, t + 1)
    nc.vector.tensor_tensor(ya, ya, g2, ALU.mult).then_inc(s.sem, s.up())
    v.wait_ge(s.sem, s.at())
    nc.vector.scalar_tensor_tensor(ya, x, ALPHA, ya, ALU.mult, ALU.add).then_inc(s.sem, s.up())
    v.wait_ge(s.sem, s.at())
    rows_norm(nc, v, s, ya, ya, r, t).then_inc(s.sem, s.up())
    v.wait_ge(s.sem, s.at())
    nc.vector.tensor_tensor(ya, ya, lng, ALU.mult).then_inc(s.sem, s.up())
    v.wait_ge(s.sem, s.at())
    return nc.vector.tensor_tensor(dst if dst is not None else x, ya, lnb, ALU.add)


def take_wait(pool, waited):
    pool.nop().then_inc(waited, 1)


def gather_experts(nc, pool, g, t, q, idx, ya, yb, landed, copied, waited):
    nc.gpsimd.tensor_copy(idx[q][:, :], g.pos[:, bass.ds(t, 1), :].rearrange("p a k -> p (a k)")).then_inc(copied, 1)
    pool.wait_ge(copied, t + 1)
    take_wait(pool, waited)
    pool.indirect_dma_start(ya[q][:, :], None, g.y[:, :], bass.IndirectOffsetOnAxis(ap=idx[q][:, 0:1], axis=0)).then_inc(landed[q], 16)
    pool.indirect_dma_start(yb[q][:, :], None, g.y[:, :], bass.IndirectOffsetOnAxis(ap=idx[q][:, 1:2], axis=0)).then_inc(landed[q], 16)


def project(nc, g, m, l):
    a = g.a
    with ExitStack() as ctx:
        sb = lambda n, s, dt=F32: ctx.enter_context(nc.sbuf_tensor(f"{n}_{l}", s, dt))
        sem = semaphores(nc, ctx, f"_proj{l}")
        psum = lambda n, s: ctx.enter_context(nc.psum_tensor(f"{n}_{l}", s, F32))
        w = sb("w_in", [P, KT, D_IN])
        if not l:
            zeros, zeros_set, y_zeroed = sb("zeros", [P, D]), sem("zeros_set"), sem("y_zeroed")
        hT = [sb(f"hT{i}", [P, KT, P]) for i in range(2)]
        xn = [sb(f"xn{i}", [P, D]) for i in range(2)]
        if l:
            yb = [sb(f"yb{i}", [P, D]) for i in range(2)]
            idx = [sb(f"idx{i}", [P, 2], I32) for i in range(2)]
            waited = sem("waited")
            g2 = sb("g2", [P, 2, D])
            ln2 = sb("ln2", [P, 2, D])
        x_norm, v_norm = Norm(sb, sem, "x_norm", D), Norm(sb, sem, "v_norm", GW)
        if l:
            c_norm = Norm(sb, sem, "c_norm", D)
        T = psum("turned", [P, KT, P])
        A, B, C, Dk = psum("bankA", [P, 512]), psum("bankB", [P, 512]), psum("bankC", [P, 4, P]), psum("bankD", [P, P])
        w_ld, vec_ld, zero = sem("w_ld"), sem("vec_ld"), sem("zeroed")
        xn_ready, turned, mod_a, mod_v = sem("xn_ready"), sem("x_turned"), sem("mod_act"), sem("mod_dve")
        a_done, b_done, c_done, d_done = sem("a_done"), sem("b_done"), sem("c_done"), sem("d_done")
        a_free, b_free, c_free, d_free = sem("a_free"), sem("b_free"), sem("c_free"), sem("d_free")
        v_step = sem("v_step")
        if l:
            landed = [sem(f"y_landed{i}") for i in range(2)]
            copied, used = sem("idx_copied"), sem("y_used")
        kv_only = lambda t: l > 0 and isinstance(t, int) and t >= LT
        stream = lambda t: 1 if isinstance(t, int) and t >= LT else 0
        LOOP = 3

        def tiles(eng, body, steps=None, per=0):
            with loop(nc, eng, 0, LOOP) as i:
                if steps:
                    steps.enter(i, per)
                for q in range(2):
                    body(i * 2 + q, q)
            if steps:
                steps.leave(LOOP)
            for t in range(2 * LOOP, NT):
                body(t, t % 2)

        with nc.Block() as block:
            @block.sync
            def _(sp):
                sp.dma_start(w[:, :, :], a["w_in"][l].rearrange("(p k) n -> p k n", k=KT)).then_inc(w_ld, 16)
                if not l:
                    sp.wait_ge(zeros_set, 1)
                    sp.dma_start(g.y[FEWEST * P:, :].rearrange("(b p) d -> p b d", p=P),
                                 across(zeros[:, :], NSLOTMAX + 1 - FEWEST)).then_inc(y_zeroed, 16)
                    sp.wait_ge(y_zeroed, 16)
                if l:
                    for s in range(2):
                        sp.dma_start(g2[:, s, :], g.mods[l - 1, s:s + 1, 5 * D:6 * D].to_broadcast([P, D])).then_inc(vec_ld, 16)
                    for j, n in enumerate(("ln2_g", "ln2_b")):
                        sp.dma_start(ln2[:, j, :], a[n][l - 1:l, :].to_broadcast([P, D])).then_inc(vec_ld, 16)

            @block.gpsimd
            def _(pool):
                if not l:
                    nc.gpsimd.memset(zeros[:, :], 0.0).then_inc(zeros_set, 1)
                for lo, hi in ((0, PAD), (PAD + SEQ, PL + PAD), (PW - PAD, PW)):
                    nc.gpsimd.memset(m.pT[:, :, lo:hi], 0.0).then_inc(zero, 1)
                for lo in (0, P + SEQ):
                    nc.gpsimd.memset(m.kT[:, lo:lo + P], 0.0).then_inc(zero, 1)
                for b in (0, LT + 1):
                    nc.gpsimd.memset(m.v[:, b, :], 0.0).then_inc(zero, 1)
                if l:
                    fetch = lambda t, q: gather_experts(nc, pool, g, t, q, idx, xn, yb, landed, copied, waited)
                    fetch(0, 0)
                    fetch(1, 1)

                def step(t, q):
                    if not (isinstance(t, int) and t >= NT - 2):
                        if l:
                            pool.wait_ge(used, t + 1)
                            pool.wait_ge(turned, t + 1)
                            fetch(t + 2, q)
                            norm_power(nc, pool, g, c_norm, t + 2)
                        norm_power(nc, pool, g, x_norm, t + 2)
                    if not kv_only(t):
                        norm_power(nc, pool, g, v_norm, t)

                for t in range(2):
                    if l:
                        norm_power(nc, pool, g, c_norm, t)
                    norm_power(nc, pool, g, x_norm, t)
                tiles(pool, step)
                pool.wait_ge(zero, 7)

            @block.vector
            def _(v):
                s = Steps(v_step)

                def normalise(t, q):
                    if l:
                        v.wait_ge(landed[q], (t - q) * 16 + 32)
                        if isinstance(t, int) and t == 0:
                            v.wait_ge(vec_ld, 64)
                        combine(nc, v, s, g, t, xn[q][:, :], yb[q][:, :], g2[:, stream(t), :], ln2[:, 0, :], ln2[:, 1, :],
                                c_norm, used, None).then_inc(s.sem, s.up())
                        v.wait_ge(s.sem, s.at())
                    x = g.x[:, bass.ds(t, 1), :].rearrange("p a d -> p (a d)")
                    rows_norm(nc, v, s, x, xn[q][:, :], x_norm, t).then_inc(xn_ready, 1)

                def modulate(t, q):
                    v.wait_ge(turned, t + 1)
                    for k in range(4, KT):
                        i = nc.vector.tensor_scalar(hT[q][:, k, :], T[:, k, :], g.cols[:, l, stream(t), 1, k:k + 1],
                                                    g.cols[:, l, stream(t), 0, k:k + 1], ALU.mult, ALU.add)
                    i.then_inc(mod_v, 1)

                def step(t, q):
                    last = isinstance(t, int) and t == NT - 1
                    if not last:
                        modulate(t + 1, 1 - q)
                    if not (isinstance(t, int) and t >= NT - 2):
                        normalise(t + 2, q)
                    v.wait_ge(c_done, t + 1)
                    kdst = (m.kT, P) if not stream(t) else (m.kcT, -LT * P)
                    pdst = PAD if not stream(t) else PL + PAD - LT * P
                    if kv_only(t):
                        nc.vector.tensor_copy(m.kcT[:, at_tile(t, P, -LT * P)], C[:, 2, :]).then_inc(c_free, 1)
                    else:
                        nc.vector.tensor_copy(m.qT[:, :, at_tile(t)], C[:, 0:2, :])
                        nc.vector.tensor_copy(kdst[0][:, at_tile(t, P, kdst[1])], C[:, 2, :])
                        nc.vector.tensor_copy(m.pT[:, 0, at_tile(t, P, pdst)], C[:, 3, :]).then_inc(c_free, 1)
                        v.wait_ge(d_done, t + 1)
                        nc.vector.tensor_copy(m.pT[:, 1, at_tile(t, P, pdst)], Dk[:, :]).then_inc(d_free, 1)
                        v.wait_ge(a_free, t + 2)
                        sg = m.sg[:, bass.ds(t, 1), :].rearrange("p a c -> p (a c)")
                        rows_norm(nc, v, s, sg, sg, v_norm, t).then_inc(s.sem, s.up())

                normalise(0, 0)
                normalise(1, 1)
                modulate(0, 0)
                nc.vector.engine_nop().then_inc(c_free, 1)
                nc.vector.engine_nop().then_inc(d_free, 1)
                tiles(v, step, s, 24 if l else 8)

            @block.scalar
            def _(act):
                def modulate(t, q):
                    act.wait_ge(turned, t + 1)
                    for k in range(4):
                        i = nc.scalar.activation(hT[q][:, k, :], T[:, k, :], ACT.Identity,
                                                 bias=g.cols[:, l, stream(t), 0, k:k + 1], scale=g.cols[:, l, stream(t), 1, k:k + 1])
                    i.then_inc(mod_a, 1)

                def step(t, q):
                    if not (isinstance(t, int) and t == NT - 1):
                        modulate(t + 1, 1 - q)
                    tile = lambda x: x[:, bass.ds(t, 1), :].rearrange("p a c -> p (a c)")
                    if not kv_only(t):
                        act.wait_ge(a_done, t + 1)
                        nc.scalar.activation(tile(m.u), A[:, 0:GW], ACT.Gelu)
                        nc.scalar.activation(tile(m.sg), A[:, GW:2 * GW], ACT.Gelu).then_inc(a_free, 1)
                    act.wait_ge(b_done, t + 1)
                    vb = 1 if not stream(t) else 2
                    if not kv_only(t):
                        nc.scalar.activation(tile(m.a), B[:, 0:GW], ACT.Copy)
                    nc.scalar.activation(m.v[:, bass.ds(t + vb, 1), :].rearrange("p a c -> p (a c)"), B[:, GW:GW + P], ACT.Copy).then_inc(b_free, 1)

                act.nop().then_inc(a_free, 1)
                act.nop().then_inc(b_free, 1)
                modulate(0, 0)
                tiles(act, step)

            @block.tensor
            def _(pe):
                def turn(t, q):
                    pe.wait_ge(xn_ready, t + 1)
                    for k in range(KT):
                        i = nc.tensor.transpose(T[:, k, :], xn[q][:, k::KT], g.k[:, K_ID:K_ID + P])
                    i.then_inc(turned, 1)

                def run(out, lhsT, rhs):
                    for k in range(KT):
                        i = nc.tensor.matmul(out, lhsT(k), rhs(k), start=k == 0, stop=k == KT - 1)
                    return i

                def step(t, q):
                    pe.wait_ge(mod_a, t + 1)
                    pe.wait_ge(mod_v, t + 1)
                    if not (isinstance(t, int) and t == NT - 1):
                        turn(t + 1, 1 - q)
                    h = hT[q]
                    if not kv_only(t):
                        pe.wait_ge(a_free, t + 1)
                        run(A[:, :], lambda k: h[:, k, :], lambda k: w[:, k, C_U:D_IN]).then_inc(a_done, 1)
                    pe.wait_ge(b_free, t + 1)
                    if not kv_only(t):
                        run(B[:, 0:GW], lambda k: h[:, k, :], lambda k: w[:, k, C_F:C_Q])
                    run(B[:, GW:GW + P], lambda k: h[:, k, :], lambda k: w[:, k, C_V:C_P]).then_inc(b_done, 1)
                    pe.wait_ge(c_free, t + 1)
                    if not kv_only(t):
                        for j in range(2):
                            run(C[:, j, :], lambda k: w[:, k, C_Q + j * P:C_Q + (j + 1) * P], lambda k: h[:, k, :])
                    i = run(C[:, 2, :], lambda k: w[:, k, C_K:C_V], lambda k: h[:, k, :])
                    if not kv_only(t):
                        i = run(C[:, 3, :], lambda k: w[:, k, C_P:C_P + P], lambda k: h[:, k, :])
                    i.then_inc(c_done, 1)
                    if not kv_only(t):
                        pe.wait_ge(d_free, t + 1)
                        run(Dk[:, :], lambda k: w[:, k, C_P + P:C_U], lambda k: h[:, k, :]).then_inc(d_done, 1)

                turn(0, 0)
                pe.wait_ge(w_ld, 16)
                tiles(pe, step)


def transform(nc, g, m, l):
    a = g.a
    ctx_out = l < DEPTH - 1
    R, RC = SEQ // P, CTX // P
    with ExitStack() as ctx:
        sb = lambda n, s, dt=F32: ctx.enter_context(nc.sbuf_tensor(f"{n}_{l}", s, dt))
        sem = semaphores(nc, ctx, f"_trans{l}")
        psum = lambda n, s: ctx.enter_context(nc.psum_tensor(f"{n}_{l}", s, F32))
        dft, dftc = sb("dft", [P, R, 4 * P]), sb("dft_ctx", [P, RC, 2 * P])
        rope = sb("rope", [P, 2, SEQ])
        wf = sb("w_fourier", [P, 2, GW])
        wc = sb("w_chan", [P, 2, 2, GW])
        wp = sb("w_pool", [P, 2, P])
        psc = sb("pool_scale", [P, 2])
        z = sb("z", [P, 8, GW])
        zt = sb("z_tmp", [P, 12, GW])
        zc = sb("z_ctx", [P, RC, GW])
        X = sb("spectrumT", [P, 2, 2, NT * P])
        pa, pb = sb("pool_a", [P, 2, PW]), sb("pool_b", [P, 2, PW])
        edge = sb("pool_edge", [P, 2, 2, 16])
        Dp = [psum(f"dft_ps{i}", [P, 512]) for i in range(4)]
        M = [psum(f"mix_ps{i}", [P, 512]) for i in range(4)]
        wf_in, dft_in, rope_in, pool_in, wpz = sem("wf_in"), sem("dft_in"), sem("rope_in"), sem("pool_in"), sem("wp_zero")
        v_step, z_done, zc_done = sem("v_step"), sem("z_done"), sem("zc_done")
        wc_mm, wc_done = sem("wc_mm"), sem("wc_done")
        dft_mm, dft_out = sem("dft_mm"), sem("dft_out")
        rot_mm, rot_free = sem("rot_mm"), sem("rot_free")
        cos_done = sem("cos_done")
        pooled, four_mm, four_out, pl_mm, pl_out = sem("pooled"), sem("four_mm"), sem("four_out"), sem("pool_mm"), sem("pool_out")
        PARTS = {0: (0,), 4: (1,), 2: (2, 3), 6: (2, 3), 1: (4, 5), 7: (4, 5), 3: (6, 7), 5: (6, 7)}
        jobs = [(0, k1, h) for k1 in range(R) for h in range(2)]
        if ctx_out:
            jobs += [(1, k1, h) for k1 in range(RC) for h in range(2)]
        spans = [(0, 512), (512, 512)] + ([(SEQ, CTX)] if ctx_out else [])
        RUNS = [(t, n) for t in range(3) for n in range(2)]

        def qk(t, n):
            return m.qT[:, t, n * 512:n * 512 + 512] if t < 2 else m.kT[:, P + n * 512:P + n * 512 + 512]

        with nc.Block() as block:
            @block.sync
            def _(sp):
                sp.dma_start(wf[:, :, :], a["w_fourier"][l].rearrange("(h p) n -> p h n", p=P)).then_inc(wf_in, 16)
                sp.dma_start(dft[:, :, :], a["dft"]).then_inc(dft_in, 16)
                sp.dma_start(dftc[:, :, :], a["dft_ctx"]).then_inc(dft_in, 16)
                sp.dma_start(rope[:, :, :], a["rope"]).then_inc(rope_in, 16)
                sp.dma_start(psc[:, :], a["pool_scale"][l]).then_inc(pool_in, 16)
                sp.wait_ge(wpz, 1)
                for w in range(4):
                    o = w % 2 * HD
                    sp.dma_start(wp[o:o + HD, w // 2, o:o + HD], a["w_pool"][l, w]).then_inc(pool_in, 16)

            @block.gpsimd
            def _(pool):
                nc.gpsimd.memset(wp[:, :, :], 0.0).then_inc(wpz, 1)
                pool.wait_ge(rope_in, 16)
                for i, (t, n) in enumerate(RUNS):
                    pool.wait_ge(rot_mm, i + 1)
                    nc.gpsimd.tensor_tensor(qk(t, n), qk(t, n), rope[:, 0, n * 512:n * 512 + 512], ALU.mult).then_inc(cos_done, 1)

            @block.vector
            def _(v):
                s = Steps(v_step)
                c8 = float(np.sqrt(0.5))
                xr = [m.a[:, r, :] for r in range(R)]
                T = [zt[:, i, :] for i in range(12)]
                Z = [z[:, i, :] for i in range(8)]

                def two(o, x, y, op):
                    nc.vector.tensor_tensor(o, x, y, op).then_inc(s.sem, s.up())

                for i in range(4):
                    j = (0, 2, 1, 3)[i]
                    two(T[2 * i], xr[j], xr[j + 4], ALU.add)
                    two(T[2 * i + 1], xr[j], xr[j + 4], ALU.subtract)
                v.wait_ge(s.sem, s.at())
                two(T[8], T[0], T[2], ALU.add)
                two(T[9], T[4], T[6], ALU.add)
                two(Z[2], T[0], T[2], ALU.subtract)
                two(Z[3], T[6], T[4], ALU.subtract)
                two(T[10], T[5], T[7], ALU.subtract)
                two(T[11], T[5], T[7], ALU.add)
                v.wait_ge(s.sem, s.at())
                two(Z[0], T[8], T[9], ALU.add)
                two(Z[1], T[8], T[9], ALU.subtract)
                for o, x, c, y, op in ((Z[4], T[10], c8, T[1], ALU.add), (Z[5], T[11], -c8, T[3], ALU.subtract),
                                       (Z[6], T[10], -c8, T[1], ALU.add), (Z[7], T[11], -c8, T[3], ALU.add)):
                    nc.vector.scalar_tensor_tensor(o, x, c, y, ALU.mult, op).then_inc(s.sem, s.up())
                v.wait_ge(s.sem, s.at())
                if ctx_out:
                    nc.vector.tensor_tensor(zc[:, 1, :], m.a[:, LT, :], m.a[:, LT + 1, :], ALU.subtract).then_inc(z_done, 1)
                    nc.vector.tensor_tensor(zc[:, 0, :], m.a[:, LT, :], m.a[:, LT + 1, :], ALU.add).then_inc(z_done, 1)
                else:
                    nc.vector.engine_nop().then_inc(z_done, 2)

                v.wait_ge(wc_mm, 1)
                nc.vector.tensor_copy(wc[:, :, :, :].rearrange("p h c n -> p (h c n)").rearrange("p (b n) -> p b n", b=2)[:, 0, :], M[0][:, :]).then_inc(wc_done, 1)
                nc.vector.tensor_copy(wc[:, :, :, :].rearrange("p h c n -> p (h c n)").rearrange("p (b n) -> p b n", b=2)[:, 1, :], M[1][:, :]).then_inc(wc_done, 1)

                p, A, B = m.pT, pa, pb
                streams = [(PAD, SEQ)] + ([(PL + PAD, CTX)] if ctx_out else [])

                def halves(o, x, lo, hi, sh, rows, t):
                    for base, n in streams:
                        b0, b1 = base - lo, base + n + hi
                        nc.vector.tensor_tensor(o[rows, t, b0:b1], x[rows, t, b0 - sh[0]:b1 - sh[0]], x[rows, t, b0 + sh[1]:b1 + sh[1]],
                                                ALU.add).then_inc(s.sem, s.up())
                every, upper = slice(0, P), slice(HD, P)
                for t in range(2):
                    halves(A, p, 7, 7, (1, 0), every, t)
                v.wait_ge(s.sem, s.at())
                halves(B, A, 6, 6, (1, 1), upper, 0)
                halves(B, A, 6, 6, (1, 1), every, 1)
                v.wait_ge(s.sem, s.at())
                halves(A, B, 4, 4, (2, 2), every, 1)
                v.wait_ge(s.sem, s.at())
                halves(B, A, 0, 0, (4, 4), upper, 1)
                v.wait_ge(s.sem, s.at())
                low = slice(0, HD)
                ends = [(0, PAD, 0), (0, PAD + SEQ - 8, 8)]
                if ctx_out:
                    ends += [(1, PL + PAD, 0), (1, PL + PAD + CTX - 8, 8)]
                for rows, src in ((low, A), (upper, B)):
                    for st, c0, e0 in ends:
                        nc.vector.tensor_tensor(edge[rows, st, :, e0:e0 + 8], src[rows, :, c0:c0 + 8],
                                                g.k[rows, K_EDGE:K_EDGE + 32].rearrange("p (t e) -> p t e", t=2)[:, :, e0:e0 + 8],
                                                ALU.mult).then_inc(s.sem, s.up())
                v.wait_ge(s.sem, s.at())
                for rows, src in ((low, A), (upper, B)):
                    for t in range(2):
                        for c0, n in streams:
                            nc.vector.scalar_tensor_tensor(A[rows, t, c0:c0 + n], src[rows, t, c0:c0 + n], g.k[rows, K_IW + t:K_IW + t + 1],
                                                           p[rows, t, c0:c0 + n], ALU.mult, ALU.subtract).then_inc(s.sem, s.up())
                v.wait_ge(s.sem, s.at())
                for n, (st, c0, e0) in enumerate(ends):
                    nc.vector.tensor_tensor(A[:, :, c0:c0 + 8], edge[:, st, :, e0:e0 + 8], p[:, :, c0:c0 + 8],
                                            ALU.subtract).then_inc(pooled, 1)

                v.wait_ge(rope_in, 16)
                for i, (t, n) in enumerate(RUNS):
                    v.wait_ge(rot_mm, i + 1)
                    if i:
                        v.wait_ge(s.sem, s.at())
                    r = M[2 + i % 2]
                    nc.vector.tensor_tensor(pb[:, 0, 0:512] if i % 2 else pb[:, 1, 0:512], r[:, :], rope[:, 1, n * 512:n * 512 + 512],
                                            ALU.mult).then_inc(rot_free, 1)
                    v.wait_ge(rot_free, i + 3)
                    v.wait_ge(cos_done, i + 1)
                    nc.vector.tensor_tensor(qk(t, n), qk(t, n), pb[:, 0, 0:512] if i % 2 else pb[:, 1, 0:512], ALU.add).then_inc(s.sem, s.up())

            @block.scalar
            def _(act):
                for i, (st, k1, h) in enumerate(jobs):
                    act.wait_ge(dft_mm, i + 1)
                    dst = X[:, h, :, k1:SEQ:R] if st == 0 else X[:, h, :, SEQ + k1:SEQ + CTX:RC]
                    nc.scalar.activation(dst, Dp[i % 4][:, 0:2 * P].rearrange("p (c n) -> p c n", c=2), ACT.Copy).then_inc(dft_out, 1)
                act.wait_ge(pool_in, 80)
                for i, (t, (c0, n)) in enumerate([(t, sp_) for t in range(2) for sp_ in spans]):
                    act.wait_ge(pl_mm, i + 1)
                    o = c0 + (PAD if c0 < SEQ else 3 * PAD)
                    nc.scalar.activation(m.pT[:, t, o:o + n], Dp[i % 4][:, 0:n], ACT.Copy, scale=psc[:, t:t + 1]).then_inc(pl_out, 1)
                for i, (h, (c0, n)) in enumerate([(h, sp_) for h in range(2) for sp_ in spans]):
                    act.wait_ge(four_mm, i + 1)
                    nc.scalar.activation(m.four[:, h, c0:c0 + n], M[i % 2][:, 0:n], ACT.Copy).then_inc(four_out, 1)

            @block.tensor
            def _(pe):
                pe.wait_ge(wf_in, 16)
                for h in range(2):
                    for c in range(2):
                        mm = nc.tensor.matmul(M[h][:, c * GW:(c + 1) * GW], g.k[:, (K_CD, K_SD)[c]:(K_CD, K_SD)[c] + P], wf[:, h, :],
                                              start=True, stop=True)
                mm.then_inc(wc_mm, 1)
                pe.nop().then_inc(rot_free, 2)
                for i, (t, n) in enumerate(RUNS):
                    pe.wait_ge(rot_free, i + 1)
                    nc.tensor.matmul(M[2 + i % 2][:, :], g.k[:, K_ROT:K_ROT + P], qk(t, n), start=True, stop=True).then_inc(rot_mm, 1)
                pe.wait_ge(dft_in, 32)
                pe.wait_ge(z_done, 2)
                for i, (st, k1, h) in enumerate(jobs):
                    if i >= 4:
                        pe.wait_ge(dft_out, i - 3)
                    o = Dp[i % 4][:, 0:2 * P]
                    if st:
                        mm = nc.tensor.matmul(o, zc[:, k1, h * P:(h + 1) * P], dftc[:, k1, :], start=True, stop=True)
                    else:
                        parts = PARTS[k1]
                        for j, zi in enumerate(parts):
                            mm = nc.tensor.matmul(o, z[:, zi, h * P:(h + 1) * P], dft[:, k1, 2 * P * j:2 * P * (j + 1)],
                                                  start=j == 0, stop=j == len(parts) - 1)
                    mm.then_inc(dft_mm, 1)
                pe.wait_ge(pooled, 4 if ctx_out else 2)
                pe.wait_ge(pool_in, 80)
                pe.wait_ge(dft_out, len(jobs))
                for i, (t, (c0, n)) in enumerate([(t, sp_) for t in range(2) for sp_ in spans]):
                    if i >= 4:
                        pe.wait_ge(pl_out, i - 3)
                    o = c0 + (PAD if c0 < SEQ else 3 * PAD)
                    nc.tensor.matmul(Dp[i % 4][:, 0:n], wp[:, t, :], pa[:, t, o:o + n], start=True, stop=True).then_inc(pl_mm, 1)
                pe.wait_ge(wc_done, 2)
                for i, (h, (c0, n)) in enumerate([(h, sp_) for h in range(2) for sp_ in spans]):
                    if i >= 2:
                        pe.wait_ge(four_out, i - 1)
                    for j in range(4):
                        mm = nc.tensor.matmul(M[i % 2][:, 0:n], wc[:, j // 2, j % 2, h * P:(h + 1) * P], X[:, j // 2, j % 2, c0:c0 + n],
                                              start=j == 0, stop=j == 3)
                    mm.then_inc(four_mm, 1)


PER_B = 50


def attend(nc, g, m, l):
    a = g.a
    N = NT if l < DEPTH - 1 else LT
    BW = 3 * P
    KW = BW + CTX
    with ExitStack() as ctx:
        sb = lambda n, s, dt=F32: ctx.enter_context(nc.sbuf_tensor(f"{n}_{l}", s, dt))
        sem = semaphores(nc, ctx, f"_att{l}")
        psum = lambda n, s: ctx.enter_context(nc.psum_tensor(f"{n}_{l}", s, F32))
        wo = sb("w_out", [P, KT, D])
        wr = sb("w_router", [P, KT, NR])
        ws = sb("w_sguT", [P, NH, P])
        bs, sink = sb("b_sgu", [P, NH]), sb("sink", [P, NH])
        vec = sb("mod2", [P, 3, D])
        ln1 = sb("ln1", [P, 2, D])
        qs = [sb(f"q_head{i}", [P, NH, P]) for i in range(2)]
        pr = [sb(f"probs{i}", [P, 2, KW]) for i in range(2)]
        pT = sb("probsT", [P, 2, KW // P, P])
        nm, sums, sd, se = sb("neg_max", [P, NH]), sb("sums", [P, 2, NH]), sb("sink_diff", [P, NH]), sb("sink_exp", [P, NH])
        mx, mx2, den = sb("max_local", [P, 2]), sb("max_ctx", [P, 2]), sb("denominator", [P, NH])
        os = sb("heads_tok", [P, 2, GW])
        ys = [sb(f"mixT{i}", [P, KT, P]) for i in range(2)]
        hb = [sb(f"h2_{i}", [P, D]) for i in range(2)]
        hT = sb("h2T", [P, KT, P])
        S = psum("scores", [P, 2, 512])
        SC = psum("scores_ctx", [P, 2, CTX])
        T = [psum(f"turn{i}", [P, 4, P]) for i in range(2)]
        O = psum("head_out", [P, 2, GW])
        Y = psum("proj", [P, 2, 512])
        R = O[:, 0, 0:NR]
        n1, n2 = Norm(sb, sem, "norm1", D), Norm(sb, sem, "norm2", D)
        e = Core()
        e.scored, e.maxed, e.expd, e.pt_full, e.pt_free, e.pv_done, e.o_ready = (
            sem(n) for n in ("scored", "maxed", "expd", "pt_full", "pt_free", "pv_done", "o_ready"))
        e.o_turned, e.o_free, e.fp_ready, e.q_ready, e.y0_full, e.y1_full, e.y_used = (
            sem(n) for n in ("o_turned", "o_free", "fp_ready", "q_ready", "y0_full", "y1_full", "y_used"))
        e.norm2_done, e.scaled2, e.h2_ready, e.h2a_full, e.h2b_full, e.h2T_ready, e.r_full = (
            sem(n) for n in ("norm2_done", "scaled2", "h2_ready", "h2a_full", "h2b_full", "h2T_ready", "r_full"))
        e.r_used, e.v_step, e.w_in, e.vec_in, e.small_in, e.vec_free, e.one_added = (
            sem(n) for n in ("r_used", "v_step", "w_in", "vec_in", "small_in", "vec_free", "one_added"))
        stored = [sem(f"h2_stored{i}") for i in range(2)]
        is_ctx = lambda t: isinstance(t, int) and t >= LT
        LOOP = (1, 3)

        def iterations(eng, body, steps=None, per=0):
            for t in range(2 * LOOP[0]):
                body(t, t % 2)
            with loop(nc, eng, *LOOP) as i:
                if steps:
                    steps.enter(i - LOOP[0], per)
                for q in range(2):
                    body(i * 2 + q, q)
            if steps:
                steps.leave(LOOP[1] - LOOP[0])
            for t in range(2 * LOOP[1], N + 2):
                body(t, t % 2)

        att = lambda t: not isinstance(t, int) or t < N
        prj = lambda t: not isinstance(t, int) or 1 <= t <= N
        rtr = lambda t: not isinstance(t, int) or t >= 2
        known = lambda t, lo: not isinstance(t, int) or t >= lo

        with nc.Block() as block:
            @block.sync
            def _(sp):
                sp.dma_start(ws[:, :, :], a["w_sgu"][l]).then_inc(e.small_in, 16)
                sp.dma_start(bs[:, :], a["b_sgu"][l]).then_inc(e.small_in, 16)
                sp.dma_start(sink[:, :], a["attn_sink"][l:l + 1, :].to_broadcast([P, NH])).then_inc(e.small_in, 16)
                sp.dma_start(wr[:, :, 0:NG], a["w_router_group"][l].rearrange("(k p) n -> p k n", p=P)).then_inc(e.small_in, 16)
                sp.dma_start(wr[:, :, NG:NR], a["w_router_expert"][l].rearrange("(k p) g n -> p k (g n)", p=P)).then_inc(e.small_in, 16)
                sp.dma_start(wo[:, :, :], a["w_out"][l].rearrange("(k p) n -> p k n", p=P)).then_inc(e.w_in, 16)
                for j, n in enumerate(("ln1_g", "ln1_b")):
                    sp.dma_start(ln1[:, j, :], a[n][l:l + 1, :].to_broadcast([P, D])).then_inc(e.vec_in, 16)

                def vectors(s):
                    for j, c in enumerate((2, 3, 4)):
                        sp.dma_start(vec[:, j, :], g.mods[l, s:s + 1, c * D:(c + 1) * D].to_broadcast([P, D])).then_inc(e.vec_in, 16)

                def step(t, q):
                    if prj(t):
                        sp.wait_ge(e.h2_ready, t)
                        sp.dma_start(g.h2[at_tile(t - 1), :], hb[1 - q][:, :]).then_inc(stored[1 - q], 16)
                        if isinstance(t, int) and t == LT and N > LT:
                            sp.wait_ge(e.vec_free, 1)
                            vectors(1)

                vectors(0)
                iterations(sp, step)
                for i in range(2):
                    sp.wait_ge(stored[i], 16 * N // 2)

            @block.gpsimd
            def _(pool):

                def add_one(s):
                    pool.wait_ge(e.vec_in, 80 if s == 0 else 128)
                    nc.gpsimd.tensor_scalar(vec[:, 2, :], vec[:, 2, :], 1.0, None, ALU.add).then_inc(e.one_added, 1)
                    pool.wait_ge(e.one_added, s + 1)

                add_one(0)
                def step(t, q):
                    if att(t):
                        attention_part(t, q)
                    if prj(t):
                        norm_power(nc, pool, g, n1, t - 1)
                        norm_power(nc, pool, g, n2, t - 1)
                        modulate_part(t, q)

                def attention_part(t, q):
                    if known(t, 2):
                        pool.wait_ge(e.scored, t * 2 - 2)
                    for kv in range(NKV):
                        own_rows = g.k[:, K_KV + kv:K_KV + kv + 1].unsqueeze(2).to_broadcast([P, 2, P])
                        i = nc.gpsimd.tensor_tensor(qs[q][:, 2 * kv:2 * kv + 2, :], m.qT[:, :, at_tile(t)], own_rows, ALU.mult)
                    i.then_inc(e.q_ready, 1)
                    if known(t, 2):
                        pool.wait_ge(e.y1_full, t - 1)
                    nc.gpsimd.tensor_copy(ys[q][:, 4:6, :], m.four[:, :, at_tile(t)])
                    o = PAD if not is_ctx(t) else 3 * PAD
                    nc.gpsimd.tensor_copy(ys[q][:, 6:8, :], m.pT[:, :, at_tile(t, P, o)]).then_inc(e.fp_ready, 1)

                def modulate_part(t, q):
                    if isinstance(t, int) and t == LT + 1:
                        add_one(1)
                    h = hb[1 - q]
                    pool.wait_ge(e.norm2_done, t)
                    nc.gpsimd.tensor_tensor(h[:, :], h[:, :], vec[:, 2, :], ALU.mult).then_inc(e.scaled2, 1)
                    pool.wait_ge(e.scaled2, t)
                    nc.gpsimd.tensor_tensor(h[:, :], h[:, :], vec[:, 1, :], ALU.add).then_inc(e.h2_ready, 1)
                    if isinstance(t, int) and t == LT:
                        pool.wait_ge(e.h2_ready, LT)
                        nc.gpsimd.engine_nop().then_inc(e.vec_free, 1)

                iterations(pool, step)

            @block.vector
            def _(v):
                s = Steps(e.v_step)
                small = lambda i: i.then_inc(s.sem, s.up())

                def maxima(t, pair):
                    v.wait_ge(e.scored, t * 2 + pair + 1)
                    h = slice(2 * pair, 2 * pair + 2)
                    if not is_ctx(t):
                        kind = 1 if not isinstance(t, int) else 0 if t == 0 else 2 if t == LT - 1 else 1
                        mask = g.k[:, K_MASK + kind * 2 * P:K_MASK + (kind + 1) * 2 * P].rearrange("p (s j) -> p s j", s=2)
                        for i in range(2):
                            own = S[:, i, 0:4 * P].rearrange("p (s w j) -> p s w j", s=2, w=2)[:, :, 0, :]
                            small(nc.vector.tensor_tensor(own, own, mask, ALU.add))
                        v.wait_ge(s.sem, s.at())
                        small(nc.vector.tensor_reduce(mx[:, :], S[:, :, 0:BW], AX, ALU.max))
                    if pair or known(t, 1):
                        v.wait_ge(e.maxed, t * 4 + pair * 2)
                    small(nc.vector.tensor_reduce(mx2[:, :], SC[:, :, :], AX, ALU.max))
                    v.wait_ge(s.sem, s.at())
                    if not is_ctx(t):
                        small(nc.vector.tensor_tensor(mx2[:, :], mx[:, :], mx2[:, :], ALU.max))
                        v.wait_ge(s.sem, s.at())
                    small(nc.vector.scalar_tensor_tensor(mx2[:, :], mx2[:, :], SCALE, sink[:, h], ALU.mult, ALU.max))
                    v.wait_ge(s.sem, s.at())
                    nc.vector.tensor_scalar(nm[:, h], mx2[:, :], -1.0, None, ALU.mult).then_inc(e.maxed, 1)
                    nc.vector.tensor_tensor(sd[:, h], sink[:, h], mx2[:, :], ALU.subtract).then_inc(e.maxed, 1)

                def heads(t, q):
                    if known(t, 1):
                        v.wait_ge(e.o_turned, t)
                    v.wait_ge(e.pv_done, t * 2 + 2)
                    b = over(bs[:, :], HD)
                    r4 = lambda x: x.rearrange("p (h c) -> p h c", h=NH)
                    small(nc.vector.tensor_tensor(r4(os[:, 1, :]), r4(O[:, 1, :]), b, ALU.add))
                    v.wait_ge(s.sem, s.at())
                    small(nc.vector.tensor_tensor(os[:, 1, :], os[:, 1, :], m.u[:, bass.ds(t, 1), :].rearrange("p a c -> p (a c)"), ALU.mult))
                    v.wait_ge(e.expd, t * 2 + 2)
                    small(nc.vector.tensor_tensor(den[:, :], sums[:, 1, :], se[:, :], ALU.add))
                    v.wait_ge(s.sem, s.at())
                    if not is_ctx(t):
                        small(nc.vector.tensor_tensor(den[:, :], den[:, :], sums[:, 0, :], ALU.add))
                        v.wait_ge(s.sem, s.at())
                    small(nc.vector.reciprocal(den[:, :], den[:, :]))
                    v.wait_ge(s.sem, s.at())
                    nc.vector.tensor_tensor(r4(os[:, 0, :]), r4(O[:, 0, :]), over(den[:, :], HD), ALU.mult).then_inc(e.o_ready, 1)

                def step(t, q):
                    if att(t):
                        maxima(t, 0)
                    if rtr(t):
                        v.wait_ge(e.h2a_full, t - 1)
                        if known(t, 3):
                            v.wait_ge(e.r_full, t - 2)
                        nc.vector.tensor_copy(hT[:, 0:4, :], T[1][:, :, :]).then_inc(e.h2T_ready, 1)
                        v.wait_ge(e.h2b_full, t - 1)
                        nc.vector.tensor_copy(hT[:, 4:8, :], T[0][:, :, :]).then_inc(e.h2T_ready, 1)
                    if att(t):
                        maxima(t, 1)
                    if prj(t):
                        u, h = t - 1, hb[1 - q]
                        x = g.x[:, bass.ds(t - 1, 1), :].rearrange("p a d -> p (a d)")
                        if isinstance(t, int) and t in (1, LT + 1):
                            v.wait_ge(e.vec_in, 80 if t == 1 else 128)
                        if known(t, 3):
                            v.wait_ge(stored[1 - q], (t - 1 - (1 - q)) * 8)
                            v.wait_ge(e.h2b_full, t - 2)
                        v.wait_ge(e.y1_full, t)
                        nc.vector.tensor_tensor(h[:, :], Y[:, :, :].rearrange("p a n -> p (a n)"), vec[:, 0, :], ALU.mult).then_inc(e.y_used, 1)
                        v.wait_ge(e.y_used, t)
                        small(nc.vector.scalar_tensor_tensor(x, x, ALPHA, h[:, :], ALU.mult, ALU.add))
                        v.wait_ge(s.sem, s.at())
                        small(rows_norm(nc, v, s, x, x, n1, u))
                        v.wait_ge(s.sem, s.at())
                        small(nc.vector.tensor_tensor(x, x, ln1[:, 0, :], ALU.mult))
                        v.wait_ge(s.sem, s.at())
                        small(nc.vector.tensor_tensor(x, x, ln1[:, 1, :], ALU.add))
                    if att(t):
                        heads(t, q)
                    if prj(t):
                        v.wait_ge(s.sem, s.at())
                        rows_norm(nc, v, s, x, h[:, :], n2, u).then_inc(e.norm2_done, 1)

                v.wait_ge(e.small_in, 80)
                iterations(v, step, s, PER_B)

            @block.scalar
            def _(act):
                def exps(t, pair):
                    act.wait_ge(e.maxed, t * 4 + pair * 2 + 2)
                    if known(t, 1):
                        act.wait_ge(e.pt_full, t * 6 + 3 * pair - 3)
                        if pair == 0:
                            act.wait_ge(e.o_ready, t)
                    for i in range(2):
                        h = 2 * pair + i
                        if not is_ctx(t):
                            nc.scalar.activation(pr[pair][:, i, 0:BW], S[:, i, 0:BW], ACT.Exp, bias=nm[:, h:h + 1], scale=SCALE,
                                                 accum_out=sums[:, 0, h:h + 1])
                        nc.scalar.activation(pr[pair][:, i, BW:KW], SC[:, i, :], ACT.Exp, bias=nm[:, h:h + 1], scale=SCALE,
                                             accum_out=sums[:, 1, h:h + 1])
                    nc.scalar.activation(se[:, 2 * pair:2 * pair + 2], sd[:, 2 * pair:2 * pair + 2], ACT.Exp).then_inc(e.expd, 1)

                def copy_turned(t, pair):
                    flat = pT[:, :, :, :].rearrange("p a j n -> p (a j) n")
                    if pair or known(t, 1):
                        act.wait_ge(e.pv_done, t * 2 + pair)
                    if is_ctx(t):
                        act.wait_ge(e.pt_full, t * 6 + pair * 3 + 3)
                        nc.scalar.activation(pT[:, :, 3:5, :], T[1 - pair][:, :, :].rearrange("p (a j) n -> p a j n", a=2),
                                             ACT.Copy).then_inc(e.pt_free, 3)
                        return
                    for j in range(3):
                        lo, hi = 4 * j, min(4 * j + 4, 10)
                        act.wait_ge(e.pt_full, t * 6 + pair * 3 + j + 1)
                        nc.scalar.activation(flat[:, lo:hi, :], T[(1 + pair + j) % 2][:, 0:hi - lo, :], ACT.Copy).then_inc(e.pt_free, 1)

                def step(t, q):
                    if prj(t):
                        act.wait_ge(e.o_turned, t)
                        if known(t, 3):
                            act.wait_ge(e.y1_full, t - 2)
                        nc.scalar.activation(ys[1 - q][:, 0:4, :], T[0][:, :, :], ACT.Copy).then_inc(e.o_free, 1)
                    if att(t):
                        exps(t, 0)
                        copy_turned(t, 0)
                        exps(t, 1)
                    if rtr(t):
                        act.wait_ge(e.r_full, t - 1)
                        nc.scalar.activation(g.logits[:, bass.ds(t - 2, 1), :].rearrange("p a n -> p (a n)"), R, ACT.Copy).then_inc(e.r_used, 1)
                    if att(t):
                        copy_turned(t, 1)

                iterations(act, step)

            @block.tensor
            def _(pe):
                ident = g.k[:, K_ID:K_ID + P]

                def scores(t, q, pair):
                    if pair or known(t, 1):
                        pe.wait_ge(e.expd, t * 2 + pair)
                    for i in range(2):
                        qh = qs[q][:, 2 * pair + i, :]
                        if not is_ctx(t):
                            keys = m.kT[:, bass.ds(t * P, BW)] if not isinstance(t, int) else m.kT[:, t * P:t * P + BW]
                            nc.tensor.matmul(S[:, i, 0:BW], qh, keys, start=True, stop=True)
                        mm = nc.tensor.matmul(SC[:, i, :], qh, m.kcT[:, :], start=True, stop=True)
                    mm.then_inc(e.scored, 1)

                def turn_probs(t, pair):
                    pe.wait_ge(e.expd, t * 2 + pair + 1)
                    flat = pr[pair][:, :, :].rearrange("p a n -> p (a n)")
                    blocks = [[0, 1, 2, 3], [4, 5, 6, 7], [8, 9]] if not is_ctx(t) else [[3, 4, 8, 9]]
                    for j, group in enumerate(blocks):
                        if pair == 0 and j == 0:
                            if rtr(t):
                                pe.wait_ge(e.h2T_ready, t * 2 - 3)
                            elif t == 1:
                                pe.wait_ge(e.pt_free, 6)
                        elif pair == 0 and j == 1:
                            if rtr(t):
                                pe.wait_ge(e.h2T_ready, t * 2 - 2)
                            elif t == 1:
                                pe.wait_ge(e.o_free, 1)
                        else:
                            pe.wait_ge(e.pt_free, t * 6 + 3 * pair + j - 1)
                            if pair == 1 and j == 0 and is_ctx(t):
                                pe.wait_ge(e.h2T_ready, t * 2 - 2)
                        for n, b in enumerate(group):
                            tr = nc.tensor.transpose(T[(1 + pair + j) % 2][:, n, :], flat[:, b * P:(b + 1) * P], ident)
                        tr.then_inc(e.pt_full, 3 if is_ctx(t) else 1)

                def values(t, pair):
                    pe.wait_ge(e.pt_free, t * 6 + 3 * pair + 3)
                    if pair == 0 and known(t, 1):
                        pe.wait_ge(e.o_ready, t)
                    for i in range(2):
                        js = range(5) if not is_ctx(t) else (3, 4)
                        for j in js:
                            block = t + j if j < 3 else LT + 2 + j - 3
                            v = m.v[:, bass.ds(block, 1), :].rearrange("p a c -> p (a c)")[:, pair * HD:(pair + 1) * HD]
                            h = 2 * pair + i
                            mm = nc.tensor.matmul(O[:, 0, h * HD:(h + 1) * HD], pT[:, i, j, :], v, start=j == js[0], stop=j == 4)
                    mm.then_inc(e.pv_done, 1)

                def gate(t):
                    sg = m.sg[:, bass.ds(t, 1), :].rearrange("p a c -> p (a c)")
                    if known(t, 1):
                        pe.wait_ge(e.o_ready, t)
                    if rtr(t):
                        pe.wait_ge(e.r_used, t - 1)
                    for h in range(NH):
                        nc.tensor.matmul(O[:, 1, h * HD:(h + 1) * HD], ws[:, h, :], sg[:, h * HD:(h + 1) * HD], start=True, stop=True)

                def project_half(t, q, half):
                    if half == 0:
                        pe.wait_ge(e.o_free, t)
                        pe.wait_ge(e.fp_ready, t)
                        if known(t, 2):
                            pe.wait_ge(e.y_used, t - 1)
                    for j, k in enumerate((2, 3, 6, 7, 0, 1, 4, 5)):
                        mm = nc.tensor.matmul(Y[:, half, :], ys[1 - q][:, j, :], wo[:, k, half * 512:(half + 1) * 512], start=j == 0, stop=j == KT - 1)
                    mm.then_inc((e.y0_full, e.y1_full)[half], 1)

                def step(t, q):
                    if prj(t):
                        pe.wait_ge(e.o_ready, t)
                        pe.wait_ge(e.pt_free, t * 6)
                        for j in range(4):
                            tr = nc.tensor.transpose(T[0][:, j, :], os[:, j // 2, j % 2 * P:(j % 2 + 1) * P], ident)
                        tr.then_inc(e.o_turned, 1)
                    if att(t):
                        pe.wait_ge(e.q_ready, t + 1)
                        scores(t, q, 0)
                    if prj(t):
                        project_half(t, q, 0)
                    if rtr(t):
                        pe.wait_ge(e.h2_ready, t - 1)
                        for j in range(4):
                            tr = nc.tensor.transpose(T[1][:, j, :], hb[q][:, j * P:(j + 1) * P], ident)
                        tr.then_inc(e.h2a_full, 1)
                        if prj(t):
                            pe.wait_ge(e.o_free, t)
                        for j in range(4):
                            tr = nc.tensor.transpose(T[0][:, j, :], hb[q][:, (j + 4) * P:(j + 5) * P], ident)
                        tr.then_inc(e.h2b_full, 1)
                    if att(t):
                        turn_probs(t, 0)
                        scores(t, q, 1)
                    if rtr(t):
                        pe.wait_ge(e.h2T_ready, t * 2 - 2)
                        pe.wait_ge(e.o_ready, t if att(t) else N)
                        if known(t, 3):
                            pe.wait_ge(e.r_used, t - 2)
                        for k in range(KT):
                            mm = nc.tensor.matmul(R, hT[:, k, :], wr[:, k, :], start=k == 0, stop=k == KT - 1)
                        mm.then_inc(e.r_full, 1)
                    if prj(t):
                        project_half(t, q, 1)
                    if att(t):
                        gate(t)
                        values(t, 0)
                        turn_probs(t, 1)
                        values(t, 1)

                pe.wait_ge(e.small_in, 80)
                pe.wait_ge(e.w_in, 16)
                iterations(pe, step)


def route_and_experts(nc, g, l):
    a = g.a
    N = NT if l < DEPTH - 1 else LT
    NB_MAX = N * P * 2 // P + NE
    NB_MIN = N * P * 2 // P
    CB = N * P // P
    with ExitStack() as ctx:
        sb = lambda n, s, dt=F32: ctx.enter_context(nc.sbuf_tensor(f"{n}_{l}", s, dt))
        sem = semaphores(nc, ctx, f"_moe{l}")
        psum = lambda n, s: ctx.enter_context(nc.psum_tensor(f"{n}_{l}", s, F32))
        G, E = g.logits[:, 0:N, 0:NG], g.logits[:, 0:N, NG:NR].rearrange("p t (g e) -> p t g e", g=NG)
        gtop, gdiff, gexp, gsum = sb("group_top", [P, N]), sb("group_diff", [P, N, NG]), sb("group_exp", [P, N, NG]), sb("group_sum", [P, N])
        gtie, goh = sb("group_tie", [P, N]), sb("group_hot", [P, N, NG])
        masked, sel = sb("masked", [P, N, NG, EPG]), sb("fine_logits", [P, N, EPG])
        top = [sb(f"fine_top{k}", [P, N]) for k in range(2)]
        tie, eoh = sb("fine_tie", [P, N]), [sb(f"fine_hot{k}", [P, N, EPG]) for k in range(2)]
        ediff, eexp, esum = sb("fine_diff", [P, N]), sb("fine_exp", [P, N]), sb("fine_sum", [P, N])
        hot = [sb(f"expert_hot{k}", [P, N, NG, EPG]) for k in range(2)]
        both = sb("expert_both", [P, N, NE])
        tot = sb("running_total", [P, N, NE])
        cmp_n, nb = sb("count_cmp", [P, NE, CB]), sb("expert_blocks", [P, NE])
        end = [sb(f"block_end{i}", [P, NE]) for i in range(2)]
        start = sb("slot_start", [P, NE])
        cmp_b = sb("block_cmp", [1, NBT, NE])
        cmp_c = sb("pair_cmp", [1, 2, NBT])
        half = sb("half_blocks", [1, 2])
        tab_f, tab = sb("table_f", [1, NBT + 2]), sb("table", [1, NBT + 2], I32)
        slot, posf = sb("slot_all", [P, N, NE]), sb("slot_f", [P, N, 2])
        zero = sb("zero_slots", [P, NBT], I32)
        waited = sem("waited")
        wg, wu, wd = ([sb(f"{n}{i}", [P, KT, DE] if n != "w_down" else [P, JT, D]) for i in range(2)] for n in ("w_gate", "w_up", "w_down"))
        idx = [sb(f"rows_idx{i}", [P, 1], I32) for i in range(2)]
        xg = [sb(f"rows{i}", [P, D]) for i in range(2)]
        xT = sb("rowsT", [P, KT, P])
        silu, hid = sb("silu", [P, 2, P]), sb("hidT", [P, JT, P])
        yo = [sb(f"y_out{i}", [P, D]) for i in range(2)]
        T = psum("rows_turned", [P, KT, P])
        H = [psum(f"gate_up{i}", [P, 4, P]) for i in range(2)]
        Y = psum("down", [P, 2, 512])
        before, total = psum("tokens_before", [P, N * NE]), psum("tile_total", [P, N * NE])
        zeroed, slots_zero = sem("zeroed"), sem("slots_zero")
        v_step, exp_in, exp_out, hot_ready, counted = sem("v_step"), sem("exp_in"), sem("exp_out"), sem("hot_ready"), sem("counted")
        table_ready, pos_ready, scattered = sem("table_ready"), sem("pos_ready"), sem("scattered")
        g_in, u_in, d_in = ([sem(f"{n}_in{i}") for i in range(2)] for n in ("gate", "up", "down"))
        idx_in, rows_in = ([sem(f"{n}_in{i}") for i in range(2)] for n in ("idx", "rows"))
        turned, xT_ready = sem("rows_turned"), sem("xT_ready")
        h_full, silu_done, hid_done = sem("h_full"), sem("silu_done"), sem("hid_done")
        y_full, y_done, stored = sem("y_full"), sem("y_done"), [sem(f"y_stored{i}") for i in range(2)]

        def blocks(eng, body):
            eng.wait_ge(table_ready, 1)
            full = eng.value_load(tab[0:1, NBT:NBT + 1], min_val=NB_MIN // 2, max_val=NB_MAX // 2)
            begun = eng.value_load(tab[0:1, NBT + 1:NBT + 2], min_val=NB_MIN // 2, max_val=(NB_MAX + 1) // 2)
            with loop(nc, eng, 0, full) as i:
                for q in range(2):
                    body(i, q)
            with eng.If_lt(eng.to_reg(full), eng.to_reg(begun)):
                body(full, 0)
            return full, begun

        with nc.Block() as block:
            @block.sync
            def _(sp):
                def weights(i, q):
                    b = i * 2 + q
                    e = sp.value_load(tab[0:1, bass.ds(b, 1)], min_val=0, max_val=NE - 1)
                    sp.wait_ge(h_full, b * 4 + 4)
                    for w, n, s in ((wg, "w_exp_gate", g_in), (wu, "w_exp_up", u_in)):
                        src = a[n][l][bass.ds(e, 1)].rearrange("a (p k) n -> p (a k) n", k=KT)
                        sp.dma_start(w[q][:, :, :], src).then_inc(s[q], 16)
                    sp.wait_ge(y_full, b * 2 + 2)
                    src = a["w_exp_down"][l][bass.ds(e, 1)].rearrange("a (j p) n -> p (a j) n", p=P)
                    sp.dma_start(wd[q][:, :, :], src).then_inc(d_in[q], 16)

                blocks(sp, weights)

            @block.gpsimd
            def _(pool):
                nc.gpsimd.memset(zero[:, :], 0).then_inc(zeroed, 1)
                pool.wait_ge(zeroed, 1)
                pool.dma_start(g.slots[l].rearrange("(p n) a -> p (n a)", p=P), zero[:, :]).then_inc(slots_zero, 16)
                pool.wait_ge(slots_zero, 16)
                pool.wait_ge(pos_ready, 2)
                for t in range(N):
                    for k in range(2):
                        pool.indirect_dma_start(g.slots[l][:, :], bass.IndirectOffsetOnAxis(ap=g.pos[:, t, k:k + 1], axis=0),
                                                g.ids[:, t:t + 1], None).then_inc(scattered, 16)
                pool.wait_ge(scattered, 16 * 2 * N)

                def fetch(b, i, q):
                    pool.dma_start(idx[q][:, :], g.slots[l][at_tile(b), :]).then_inc(idx_in[q], 16)
                    pool.wait_ge(idx_in[q], i * 16 + 16)
                    take_wait(pool, waited)
                    pool.indirect_dma_start(xg[q][:, :], None, g.h2[:, :],
                                            bass.IndirectOffsetOnAxis(ap=idx[q][:, 0:1], axis=0)).then_inc(rows_in[q], 16)

                def ahead(i, q):
                    pool.wait_ge(turned, i * 2 + q + 1)
                    fetch(i * 2 + q + 2, i + 1, q)

                fetch(0, 0, 0)
                fetch(1, 0, 1)
                full, begun = blocks(pool, ahead)
                pool.wait_ge(rows_in[0], begun * 16 + 16)
                pool.wait_ge(rows_in[1], full * 16 + 16)
                pool.wait_ge(stored[0], begun * 16 + 16)
                pool.wait_ge(stored[1], full * 16 + 16)

            @block.vector
            def _(v):
                s = Steps(v_step)
                step = lambda i: i.then_inc(s.sem, s.up())
                done = lambda: v.wait_ge(s.sem, s.at())
                tt, red, sts = nc.vector.tensor_tensor, nc.vector.tensor_reduce, nc.vector.scalar_tensor_tensor
                weight = lambda c, n: across(g.k[:, c:c + n], N)
                step(red(gtop[:, :], G, AX, ALU.max))
                done()
                step(tt(gdiff[:, :, :], G, over(gtop[:, :], NG), ALU.subtract))
                done()
                nc.vector.engine_nop().then_inc(exp_in, 1)
                step(tt(goh[:, :, :], G, over(gtop[:, :], NG), ALU.is_equal))
                done()
                step(tt(goh[:, :, :], goh[:, :, :], weight(K_GW, NG), ALU.mult))
                done()
                step(red(gtie[:, :], goh[:, :, :], AX, ALU.max))
                done()
                step(tt(goh[:, :, :], goh[:, :, :], over(gtie[:, :], NG), ALU.is_equal))
                done()
                step(tt(masked[:, :, :, :], E, over(goh[:, :, :], EPG), ALU.mult))
                done()
                step(red(sel[:, :, :], masked[:, :, :, :].rearrange("p t g e -> p t e g"), AX, ALU.add))
                done()
                for k in range(2):
                    step(red(top[k][:, :], sel[:, :, :], AX, ALU.max))
                    done()
                    step(tt(eoh[k][:, :, :], sel[:, :, :], over(top[k][:, :], EPG), ALU.is_equal))
                    done()
                    step(tt(eoh[k][:, :, :], eoh[k][:, :, :], weight(K_EW, EPG), ALU.mult))
                    done()
                    step(red(tie[:, :], eoh[k][:, :, :], AX, ALU.max))
                    done()
                    step(tt(eoh[k][:, :, :], eoh[k][:, :, :], over(tie[:, :], EPG), ALU.is_equal))
                    done()
                    for j in range(NG):
                        step(tt(hot[k][:, :, j, :], over(goh[:, :, j], EPG), eoh[k][:, :, :], ALU.mult))
                    if k == 0:
                        step(sts(sel[:, :, :], eoh[0][:, :, :], -1e38, sel[:, :, :], ALU.mult, ALU.add))
                    done()
                flat = [h[:, :, :, :].rearrange("p t g e -> p t (g e)") for h in hot]
                tt(both[:, :, :], flat[0], flat[1], ALU.add).then_inc(hot_ready, 1)
                step(tt(ediff[:, :], top[1][:, :], top[0][:, :], ALU.subtract))
                done()
                nc.vector.engine_nop().then_inc(exp_in, 1)
                r = lambda x: x[:, :].rearrange("p (t e) -> p t e", t=N)
                v.wait_ge(counted, 1)
                step(nc.vector.tensor_copy(tot[:, :, :], r(total)))
                done()
                for t in range(1, N):
                    step(tt(tot[:, t, :], tot[:, t, :], tot[:, t - 1, :], ALU.add))
                    done()
                step(sts(cmp_n[:, :, :], across(g.k[:, K_IOTA:K_IOTA + CB], NE), float(P), over(tot[:, N - 1, :], CB), ALU.mult, ALU.is_lt))
                done()
                step(red(nb[:, :], cmp_n[:, :, :], AX, ALU.add))
                done()
                src = nb
                for i in range(5):
                    sh, dst = 1 << i, end[i % 2]
                    step(nc.vector.tensor_copy(dst[:, 0:sh], src[:, 0:sh]))
                    step(tt(dst[:, sh:NE], src[:, sh:NE], src[:, 0:NE - sh], ALU.add))
                    done()
                    src = dst
                step(tt(cmp_b[:, :, :], across(src[0:1, :], NBT), over(g.k[0:1, K_IOTA:K_IOTA + NBT], NE), ALU.is_le))
                step(nc.vector.tensor_scalar(half[:, 1:2], src[0:1, NE - 1:NE], 0.5, None, ALU.mult))
                step(nc.vector.tensor_scalar(half[:, 0:1], src[0:1, NE - 1:NE], 0.5, -0.5, ALU.mult, ALU.add))
                done()
                step(tt(cmp_c[:, :, :], across(g.k[0:1, K_IOTA:K_IOTA + NBT], 2), over(half[:, :], NBT), ALU.is_lt))
                step(red(tab_f[:, 0:NBT], cmp_b[:, :, :], AX, ALU.add))
                done()
                step(red(tab_f[:, NBT:NBT + 2], cmp_c[:, :, :], AX, ALU.add))
                step(nc.vector.tensor_scalar(tab_f[:, 0:NBT], tab_f[:, 0:NBT], float(NE - 1), None, ALU.min))
                done()
                nc.vector.tensor_copy(tab[:, :], tab_f[:, :]).then_inc(table_ready, 1)
                step(tt(start[:, :], src[:, :], nb[:, :], ALU.subtract))
                step(nc.vector.tensor_copy(slot[:, 0, :], r(before)[:, 0, :]))
                step(tt(slot[:, 1:N, :], r(before)[:, 1:N, :], tot[:, 0:N - 1, :], ALU.add))
                done()
                step(sts(slot[:, :, :], across(start[:, :], N), float(P), slot[:, :, :], ALU.mult, ALU.add))
                done()
                for k in range(2):
                    step(tt(flat[k], flat[k], slot[:, :, :], ALU.mult))
                done()
                for k in range(2):
                    step(red(posf[:, :, k], flat[k], AX, ALU.add))
                done()
                for k in range(2):
                    nc.vector.tensor_copy(g.pos[:, 0:N, k], posf[:, :, k]).then_inc(pos_ready, 1)
                v.wait_ge(exp_out, 2)
                step(red(gsum[:, :], gexp[:, :, :], AX, ALU.add))
                step(nc.vector.tensor_scalar(esum[:, :], eexp[:, :], 1.0, None, ALU.add))
                done()
                step(tt(gsum[:, :], gsum[:, :], esum[:, :], ALU.mult))
                done()
                step(nc.vector.reciprocal(g.gate[:, 0:N, 0], gsum[:, :]))
                done()
                step(tt(g.gate[:, 0:N, 1], g.gate[:, 0:N, 0], eexp[:, :], ALU.mult))
                done()

                def turn_copy(b):
                    v.wait_ge(turned, b + 1)
                    for h in range(2):
                        i = nc.vector.tensor_copy(xT[:, 4 * h:4 * h + 4, :], T[:, 4 * h:4 * h + 4, :])
                    i.then_inc(xT_ready, 1)

                nc.vector.engine_nop().then_inc(hid_done, 2)

                def products(i, q):
                    b = i * 2 + q
                    for j in range(JT):
                        v.wait_ge(silu_done, b * 4 + j + 1)
                        nc.vector.tensor_tensor(hid[:, j, :], silu[:, j % 2, :], H[j % 2][:, 1, :], ALU.mult).then_inc(hid_done, 1)
                    turn_copy(b + 1)

                turn_copy(0)
                blocks(v, products)

            @block.scalar
            def _(act):
                act.wait_ge(exp_in, 1)
                nc.scalar.activation(gexp[:, :, :], gdiff[:, :, :], ACT.Exp).then_inc(exp_out, 1)
                act.wait_ge(exp_in, 2)
                nc.scalar.activation(eexp[:, :], ediff[:, :], ACT.Exp).then_inc(exp_out, 1)
                for q in range(2):
                    act.nop().then_inc(stored[q], 16)

                def outputs(i, q):
                    b = i * 2 + q
                    for j in range(JT):
                        act.wait_ge(h_full, b * 4 + j + 9)
                        nc.scalar.activation(silu[:, j % 2, :], H[j % 2][:, 0, :], ACT.Silu).then_inc(silu_done, 1)
                    act.wait_ge(stored[q], i * 16 + 16)
                    for h in range(2):
                        act.wait_ge(y_full, b * 2 + h + 5)
                        nc.scalar.activation(yo[q][:, h * 512:(h + 1) * 512], Y[:, h, :], ACT.Copy).then_inc(y_done, 1)
                    act.wait_ge(y_done, b * 2 + 4)
                    act.dma_start(g.y[at_tile(b), :], yo[q][:, :]).then_inc(stored[q], 16)

                blocks(act, outputs)

            @block.tensor
            def _(pe):
                pe.wait_ge(hot_ready, 1)
                m = both[:, :, :].rearrange("p t e -> p (t e)")
                nc.tensor.matmul(before[:, :], g.k[:, K_TRI:K_TRI + P], m, start=True, stop=True)
                nc.tensor.matmul(total[:, :], g.k[:, K_ONE:K_ONE + P], m, start=True, stop=True).then_inc(counted, 1)
                pe.nop().then_inc(h_full, 8)
                pe.nop().then_inc(y_full, 4)
                pe.nop().then_inc(y_done, 2)

                def turn(b, i, q):
                    pe.wait_ge(rows_in[q], i * 16 + 16)
                    for k in range(KT):
                        tr = nc.tensor.transpose(T[:, k, :], xg[q][:, k::KT], g.k[:, K_ID:K_ID + P])
                    tr.then_inc(turned, 1)

                def expert(i, q):
                    b = i * 2 + q
                    pe.wait_ge(xT_ready, b + 1)
                    pe.wait_ge(g_in[q], i * 16 + 16)
                    for j in range(JT):
                        pe.wait_ge(hid_done, b * 4 + j + 1)
                        for w, o in ((wg, 0), (wu, 1)):
                            if j == 0 and o == 1:
                                pe.wait_ge(u_in[q], i * 16 + 16)
                            for k in range(KT):
                                mm = nc.tensor.matmul(H[j % 2][:, o, :], w[q][:, k, j * P:(j + 1) * P], xT[:, k, :], start=k == 0, stop=k == KT - 1)
                        mm.then_inc(h_full, 1)
                    turn(b + 1, i + q, 1 - q)
                    pe.wait_ge(d_in[q], i * 16 + 16)
                    pe.wait_ge(hid_done, b * 4 + 6)
                    for h in range(2):
                        pe.wait_ge(y_done, b * 2 + h + 1)
                        for j in range(JT):
                            mm = nc.tensor.matmul(Y[:, h, :], hid[:, j, :], wd[q][:, j, h * 512:(h + 1) * 512], start=j == 0, stop=j == JT - 1)
                        mm.then_inc(y_full, 1)

                turn(0, 0, 0)
                blocks(pe, expert)


def finish(nc, g):
    l = DEPTH - 1
    with ExitStack() as ctx:
        sb = lambda n, s, dt=F32: ctx.enter_context(nc.sbuf_tensor(f"{n}_end", s, dt))
        sem = semaphores(nc, ctx, "_end")
        ya, yb = ([sb(f"y{c}{i}", [P, D]) for i in range(2)] for c in "ab")
        idx = [sb(f"idx{i}", [P, 2], I32) for i in range(2)]
        g2, ln2 = sb("g2", [P, D]), sb("ln2", [P, 2, D])
        waited = sem("waited")
        c_norm = Norm(sb, sem, "c_norm", D)
        vec_ld, copied, used, v_step, x_ready = sem("vec_ld"), sem("idx_copied"), sem("y_used"), sem("v_step"), sem("x_ready")
        landed, stored = [sem(f"y_landed{i}") for i in range(2)], sem("x_stored")
        with nc.Block() as block:
            @block.sync
            def _(sp):
                sp.dma_start(g2[:, :], g.mods[l, 0:1, 5 * D:6 * D].to_broadcast([P, D])).then_inc(vec_ld, 16)
                for j, n in enumerate(("ln2_g", "ln2_b")):
                    sp.dma_start(ln2[:, j, :], g.a[n][l:l + 1, :].to_broadcast([P, D])).then_inc(vec_ld, 16)
                for t in range(LT):
                    sp.wait_ge(x_ready, t + 1)
                    sp.dma_start(g.out[0, t * P:(t + 1) * P, :], g.x[:, t, :]).then_inc(stored, 16)
                sp.wait_ge(stored, 16 * LT)

            @block.gpsimd
            def _(pool):
                for t in range(2):
                    gather_experts(nc, pool, g, t, t, idx, ya, yb, landed, copied, waited)
                for t in range(LT):
                    norm_power(nc, pool, g, c_norm, t)
                    if t + 2 < LT:
                        pool.wait_ge(x_ready, t + 1)
                        gather_experts(nc, pool, g, t + 2, t % 2, idx, ya, yb, landed, copied, waited)

            @block.vector
            def _(v):
                s = Steps(v_step)
                v.wait_ge(vec_ld, 48)
                for t in range(LT):
                    q = t % 2
                    v.wait_ge(landed[q], (t // 2) * 32 + 32)
                    combine(nc, v, s, g, t, ya[q][:, :], yb[q][:, :], g2[:, :], ln2[:, 0, :], ln2[:, 1, :],
                            c_norm, used, None).then_inc(x_ready, 1)


def build(nc, a, out):
    g = Core()
    with ExitStack() as ctx:
        def sb(name, shape, dt=F32):
            return ctx.enter_context(nc.sbuf_tensor(name, shape, dt))

        g.a, g.out = a, out
        g.x = sb("x_res", [P, NT, D])
        g.k = sb("consts", [P, K_N])
        g.cols = sb("mod_cols", [P, DEPTH, 2, 2, KT])
        g.pos = sb("slot_of", [P, NT, 2], I32)
        g.gate = sb("gate_of", [P, NT, 2])
        g.ids = sb("token_ids", [P, NT], I32)
        g.logits = sb("logits", [P, NT, NR])
        g.mods = nc.dram_tensor("mods", [DEPTH, 2, 6 * D], F32).ap()
        g.h2 = nc.dram_tensor("h2_rows", [NT * P, D], F32).ap()
        g.slots = [nc.dram_tensor(f"slot_token{l}", [NBT * P, 1], I32).ap() for l in range(DEPTH)]
        g.y = nc.dram_tensor("expert_rows", [(NSLOTMAX + 1) * P, D], F32).ap()
        modulation(nc, g)
        for l in range(LAYERS):
            with ExitStack() as mix:
                def ms(name, shape, dt=F32):
                    return mix.enter_context(nc.sbuf_tensor(f"{name}{l}", shape, dt))
                m = Core()
                m.qT = ms("qT", [P, 2, NT * P])
                m.kT = ms("kT", [P, SEQ + 2 * P])
                m.kcT = ms("kcT", [P, CTX])
                m.v = ms("v_tok", [P, LT + 2 + CT, P])
                m.u = ms("u_tok", [P, NT, GW])
                m.sg = ms("sgu_v", [P, NT, GW])
                m.pT = ms("poolT", [P, 2, PW])
                m.a = ms("four_tok", [P, NT, GW])
                m.four = m.a[:, :, :].rearrange("p t c -> p (t c)").rearrange("p (h n) -> p h n", h=2)
                project(nc, g, m, l)
                transform(nc, g, m, l)
                attend(nc, g, m, l)
            route_and_experts(nc, g, l)
        finish(nc, g)
    return nc


_INS = ("x", "c", "ctx", "c_ctx", "w_ada", "b_ada", "w_in", "w_fourier", "attn_sink", "w_pool", "pool_scale", "w_sgu",
        "b_sgu", "w_out", "ln1_g", "ln1_b", "w_router_group", "w_router_expert", "w_exp_gate", "w_exp_up",
        "w_exp_down", "ln2_g", "ln2_b")


def kernel(**inputs):
    import concourse.bacc as bacc
    from concourse.bass_utils import run_bass_kernel_spmd

    nc = bacc.Bacc("TRN2", target_bir_lowering=False, num_devices=1)
    given = {n: np.asarray(inputs[n]) for n in _INS}
    given["w_sgu"] = given["w_sgu"].transpose(0, 3, 1, 2)
    w = given["w_in"]
    q = w[:, :, C_Q:C_K].reshape(DEPTH, D, 2, 2, HD).transpose(0, 1, 3, 2, 4).reshape(DEPTH, D, GW)
    given["w_in"] = np.concatenate([w[:, :, :C_Q], q, w[:, :, C_K:]], 2)
    given["b_sgu"] = given["b_sgu"].transpose(0, 2, 1)
    given["pool_scale"] = given["pool_scale"].reshape(DEPTH, 2, P).transpose(0, 2, 1)
    names = ("consts", "rope", "dft", "dft_ctx", "token_ids")
    given.update(zip(names, constant_tables()))
    arrays, aps = {}, {}
    for n, v in given.items():
        arrays["in_" + n] = np.ascontiguousarray(v)
        aps[n] = nc.dram_tensor("in_" + n, v.shape, mybir.dt.from_np(v.dtype), kind="ExternalInput").ap()
    out = nc.dram_tensor("out", (1, SEQ, D), F32, kind="ExternalOutput").ap()
    build(nc, aps, out)
    r = run_bass_kernel_spmd(nc, [arrays], core_ids=[0])
    return r.results[0]["out"]
```

```python
from contextlib import ExitStack

import numpy as np

import concourse.bass as bass
from concourse import mybir

F32 = mybir.dt.float32
I32 = mybir.dt.int32
ALU = mybir.AluOpType
ACT = mybir.ActivationFunctionType
AX = mybir.AxisListType.X

P = 128
D = 1024
KT = D // P
DEPTH = 2
SEQ, CTX = 1024, 256
LT, CT = SEQ // P, CTX // P
NT = LT + CT
HD = 64
NH, NKV = 4, 2
GW = D // 4
C_F, C_Q, C_K, C_V, C_P, C_U = 0, 256, 512, 640, 768, 1024
D_IN = 1536
DE = D // 2
JT = DE // P
NG, EPG = 4, 8
NE = NG * EPG
NR = NG + NE
FEWEST = LT * 2
NSLOTMAX = (NT * P * 2) // P + NE
NBT = (NSLOTMAX + 4 + 7) // 8 * 8
SCALE = float(HD) ** -0.5
ALPHA = float((2 * DEPTH) ** 0.25)
EPS = 1e-6
NEG = -1e30
PAD = 8
PL = PAD + SEQ + PAD
PW = PL + PAD + CTX + PAD

K_ID, K_TRI, K_ONE, K_ROT, K_CD, K_SD = (i * P for i in range(6))
K_MASK = 6 * P
K_EDGE = K_MASK + 3 * 2 * P
K_IW = K_EDGE + 2 * 16
K_GW = K_IW + 2
K_EW = K_GW + NG
K_IOTA = K_EW + EPG
K_NH = K_IOTA + P
K_EPS = K_NH + 1
K_NEG = K_EPS + 1
K_KV = K_NEG + 1
K_N = K_KV + NKV


def constant_tables():
    k = np.zeros((P, K_N))
    r = np.arange(P)
    k[:, K_ID:K_ID + P] = np.eye(P)
    k[:, K_TRI:K_TRI + P] = r[:, None] < r[None, :]
    k[:, K_ONE:K_ONE + P] = 1
    for m in range(P):
        if m % 32 < 16:
            k[m + 16, K_ROT + m] = -1
        else:
            k[m - 16, K_ROT + m] = 1
    ang = 2 * np.pi * np.outer(np.arange(HD), np.arange(HD)) / HD
    for b in range(2):
        s = slice(b * HD, b * HD + HD)
        k[s, K_CD + b * HD:K_CD + b * HD + HD] = np.cos(ang)
        k[s, K_SD + b * HD:K_SD + b * HD + HD] = np.sin(ang)
    full = np.full((P, P), NEG)
    before = np.where(r[None, :] >= r[:, None], 0, NEG)
    after = np.where(r[None, :] <= r[:, None], 0, NEG)
    masks = [(full, after), (before, after), (before, full)]
    k[:, K_MASK:K_EDGE] = np.concatenate([np.concatenate(m, 1) for m in masks], 1)
    for g, w in enumerate((2, 4, 8, 16)):
        p, t, n = slice(g % 2 * HD, g % 2 * HD + HD), g // 2, SEQ
        pos = np.concatenate([np.arange(8), np.arange(n - 8, n)])
        k[p, K_EDGE + 16 * t:K_EDGE + 16 * t + 16] = 1 / (np.minimum(pos + w // 2, n) - np.maximum(pos - w // 2, 0))
        k[p, K_IW + t] = 1 / w
    k[:, K_GW:K_GW + NG] = NG - np.arange(NG)
    k[:, K_EW:K_EW + EPG] = EPG - np.arange(EPG)
    k[:, K_IOTA:K_IOTA + P] = r
    k[:, K_NH] = -0.5
    k[:, K_EPS] = EPS
    k[:, K_NEG] = -1
    for h in range(NKV):
        k[h * HD:(h + 1) * HD, K_KV + h] = 1
    tok, freq = np.arange(SEQ), 10000.0 ** (-np.arange(16) / 16)
    rope = np.zeros((P, 2, SEQ))
    for m in range(P):
        place = (tok // HD if m % HD < 32 else tok % HD).astype(float)
        a = place * freq[m % 16]
        rope[m, 0], rope[m, 1] = np.cos(a), np.sin(a)

    def dft(n):
        R = n // P
        t = np.zeros((P, R, 4 * P))
        for k1 in range(R):
            a = 2 * np.pi * (np.outer(np.arange(P), k1 + R * np.arange(P)) % n) / n
            c, s = np.cos(a) / np.sqrt(n * HD), np.sin(a) / np.sqrt(n * HD)
            f = -1 if k1 > R // 2 else 1
            t[:, k1] = np.concatenate([c, -s, f * s, f * c], 1)
        return t

    ids = (np.arange(NT)[None, :] * P + r[:, None]).astype(np.int32)
    f = np.float32
    return k.astype(f), rope.astype(f), dft(SEQ).astype(f), dft(CTX)[:, :, :2 * P].astype(f).copy(), ids


class Steps:

    def __init__(self, sem):
        self.sem, self.n, self.base = sem, 0, 0

    def up(self):
        self.n += 1
        return 1

    def at(self):
        return self.base + self.n

    def enter(self, i, per):
        self.base, self.start, self.per = i * per, self.n, per

    def leave(self, times):
        assert self.n - self.start == self.per, (self.n - self.start, self.per)
        self.base, self.n = 0, self.start + times * self.per


def loop(nc, eng, start, end):
    return nc.Fori(start, end, 1, engines=bass.OrderedEngineSet([eng.engine]), hint_back_edge=True)


def over(ap, n):
    return ap.unsqueeze(ap.ndim).to_broadcast(list(ap.shape) + [n])


def across(ap, n):
    return ap.unsqueeze(1).to_broadcast([ap.shape[0], n] + list(ap.shape[1:]))


class Core:
    pass


def at_tile(t, width=P, base=0):
    return bass.ds(t * width + base, width) if not isinstance(t, int) else slice(base + t * width, base + (t + 1) * width)


def semaphores(nc, ctx, suffix):
    taken = []

    def give_back():
        nc.clear_and_free_semaphores(taken)
        nc.all_engine_barrier()
    ctx.callback(give_back)

    def sem(name):
        taken.append(nc.alloc_semaphore(name + suffix))
        return taken[-1]
    return sem


class Norm:

    def __init__(self, sb, sem, name, width):
        self.w = min(width, 512)
        self.stats, self.mv, self.rstd = sb(name + "_stats", [P, width // self.w, 6]), sb(name + "_mv", [P, 2]), sb(name + "_rstd", [P, 1])
        self.spare = sb(name + "_spare", [P, 1])
        self.var_ready, self.eps_added, self.rstd_ready = (
            sem(f"{name}_{what}") for what in ("var_ready", "eps_added", "rstd_ready"))


def norm_power(nc, pool, g, r, n):
    pool.wait_ge(r.var_ready, n + 1)
    nc.gpsimd.tensor_tensor(r.rstd[:, :], r.mv[:, 1:2], g.k[:, K_EPS:K_EPS + 1], ALU.add).then_inc(r.eps_added, 1)
    pool.wait_ge(r.eps_added, n + 1)
    nc.gpsimd.tensor_tensor(r.rstd[:, :], r.rstd[:, :], g.k[:, K_NH:K_NH + 1], ALU.pow).then_inc(r.rstd_ready, 1)


def rows_stats(nc, v, s, src, r):
    nc.vector.memset(r.spare[:, :], 0.0)
    for j in range(src.shape[-1] // r.w):
        nc.vector.bn_stats(r.stats[:, j, :], src[:, j * r.w:(j + 1) * r.w]).then_inc(s.sem, s.up())
    v.wait_ge(s.sem, s.at())
    nc.vector.memset(r.spare[:, :], 0.0)
    nc.vector.bn_aggr(r.mv[:, :], r.stats[:, :, :].rearrange("p a b -> p (a b)")).then_inc(r.var_ready, 1)


def rows_norm(nc, v, s, src, dst, r, n):
    rows_stats(nc, v, s, src, r)
    v.wait_ge(r.rstd_ready, n + 1)
    return nc.vector.tensor_scalar(dst, src, r.mv[:, 0:1], r.rstd[:, :], ALU.subtract, ALU.mult)


def modulation(nc, g):
    a = g.a
    NC = 6 * D // 512
    with ExitStack() as ctx:
        sb = lambda n, s, dt=F32: ctx.enter_context(nc.sbuf_tensor(n, s, dt))
        sem = semaphores(nc, ctx, "")
        NW = 4
        w = [sb(f"ada_w{i}", [P, KT, 512]) for i in range(NW)]
        cond = sb("cond", [P, 2, KT])
        act_c = sb("cond_silu", [P, KT, 2])
        row = sb("ada_row", [2, DEPTH, 6 * D])
        ps = [ctx.enter_context(nc.psum_tensor(f"ada_ps{i}", [P, 512], F32)) for i in range(NW)]
        c_in, k_in, b_in = sem("c_in"), sem("consts_in"), sem("bias_in")
        w_in = [sem(f"ada_w_in{i}") for i in range(NW)]
        w_used, silu_done, ps_free = sem("ada_w_used"), sem("silu_done"), sem("ada_ps_free")
        stored, cols_in, scaled = sem("mods_stored"), sem("cols_in"), sem("cols_scaled")
        CHUNKS = DEPTH * NC

        with nc.Block() as block:
            @block.sync
            def _(sp):
                sp.dma_start(cond[:, 0, :], a["c"].rearrange("a (p k) -> p (a k)", k=KT)).then_inc(c_in, 16)
                sp.dma_start(cond[:, 1, :], a["c_ctx"].rearrange("(p k) -> p k", k=KT)).then_inc(c_in, 16)
                for s in range(2):
                    sp.dma_start(row[s:s + 1, :, :], a["b_ada"].rearrange("(a l) n -> a l n", a=1)).then_inc(b_in, 16)
                for l in range(DEPTH):
                    wl = a["w_ada"][l].rearrange("(p k) n -> p k n", k=KT)
                    with loop(nc, sp, 0, NC // NW) as i:
                        for c in range(NW):
                            sp.wait_ge(w_used, i * NW + l * NC + c + 1)
                            sp.dma_start(w[c][:, :, :], wl[:, :, bass.ds(i * (NW * 512) + c * 512, 512)]).then_inc(w_in[c], 16)
                sp.dma_start(g.k[:, :], a["consts"]).then_inc(k_in, 16)
                sp.dma_start(g.ids[:, :], a["token_ids"]).then_inc(k_in, 16)
                sp.dma_start(g.x[:, 0:2, :], a["x"][0, 0:2 * P, :].rearrange("(t p) d -> p t d", p=P)).then_inc(k_in, 16)
                sp.wait_ge(k_in, 48)

            @block.scalar
            def _(act):
                act.wait_ge(c_in, 32)
                nc.scalar.activation(act_c[:, :, :].rearrange("p k s -> p s k"), cond[:, :, :], ACT.Silu).then_inc(silu_done, 1)
                for l in range(DEPTH):
                    act.wait_ge(ps_free, NW + NC * (l + 1))
                    act.dma_start(g.mods[l], row[:, l, :]).then_inc(stored, 16)
                    act.wait_ge(stored, 16 * (l + 1))
                    for s in range(2):
                        for h in range(2):
                            act.dma_start(g.cols[:, l, s, h, :],
                                          g.mods[l, s, h * D:(h + 1) * D].rearrange("(p k) -> p k", k=KT)).then_inc(cols_in, 16)

            @block.tensor
            def _(pe):
                pe.nop().then_inc(w_used, NW)
                pe.wait_ge(silu_done, 1)
                with loop(nc, pe, 0, CHUNKS // NW) as i:
                    for c in range(NW):
                        pe.wait_ge(w_in[c], i * 16 + 16)
                        pe.wait_ge(ps_free, i * NW + c + 1)
                        for k in range(KT):
                            for j in range(4):
                                mm = nc.tensor.matmul(ps[c][32 * j:32 * j + 2, 0:P], act_c[:, k, :],
                                                      w[c][:, k, j * P:(j + 1) * P], start=k == 0, stop=k == KT - 1)
                        mm.then_inc(w_used, 1)

            @block.vector
            def _(v):
                nc.vector.engine_nop().then_inc(ps_free, NW)
                v.wait_ge(b_in, 32)
                for l in range(DEPTH):
                    with loop(nc, v, 0, NC // NW) as i:
                        for c in range(NW):
                            v.wait_ge(w_used, i * NW + NC * l + c + 1 + NW)
                            for j in range(4):
                                n = row[:, l, bass.ds(i * (NW * 512) + c * 512 + j * P, P)]
                                add = nc.vector.tensor_tensor(n, ps[c][32 * j:32 * j + 2, 0:P], n, ALU.add)
                            add.then_inc(ps_free, 1)
                v.wait_ge(cols_in, 16 * 8)
                nc.vector.tensor_scalar(g.cols[:, :, :, 1, :], g.cols[:, :, :, 1, :], 1.0, None, ALU.add).then_inc(scaled, 1)
                v.wait_ge(scaled, 1)


def combine(nc, v, s, g, t, ya, yb, g2, lng, lnb, r, used, dst):
    x = g.x[:, bass.ds(t, 1), :].rearrange("p a d -> p (a d)")
    gate = g.gate[:, bass.ds(t, 1), :].rearrange("p a d -> p (a d)")
    nc.vector.tensor_scalar(ya, ya, gate[:, 0:1], None, ALU.mult).then_inc(s.sem, s.up())
    v.wait_ge(s.sem, s.at())
    nc.vector.scalar_tensor_tensor(ya, yb, gate[:, 1:2], ya, ALU.mult, ALU.add).then_inc(used, 1)
    v.wait_ge(used, t + 1)
    nc.vector.tensor_tensor(ya, ya, g2, ALU.mult).then_inc(s.sem, s.up())
    v.wait_ge(s.sem, s.at())
    nc.vector.scalar_tensor_tensor(ya, x, ALPHA, ya, ALU.mult, ALU.add).then_inc(s.sem, s.up())
    v.wait_ge(s.sem, s.at())
    rows_norm(nc, v, s, ya, ya, r, t).then_inc(s.sem, s.up())
    v.wait_ge(s.sem, s.at())
    nc.vector.tensor_tensor(ya, ya, lng, ALU.mult).then_inc(s.sem, s.up())
    v.wait_ge(s.sem, s.at())
    return nc.vector.tensor_tensor(dst if dst is not None else x, ya, lnb, ALU.add)


def take_wait(pool, waited):
    pool.nop().then_inc(waited, 1)


def gather_experts(nc, pool, g, t, q, idx, ya, yb, landed, copied, waited):
    nc.gpsimd.tensor_copy(idx[q][:, :], g.pos[:, bass.ds(t, 1), :].rearrange("p a k -> p (a k)")).then_inc(copied, 1)
    pool.wait_ge(copied, t + 1)
    take_wait(pool, waited)
    pool.indirect_dma_start(ya[q][:, :], None, g.y[:, :], bass.IndirectOffsetOnAxis(ap=idx[q][:, 0:1], axis=0)).then_inc(landed[q], 16)
    pool.indirect_dma_start(yb[q][:, :], None, g.y[:, :], bass.IndirectOffsetOnAxis(ap=idx[q][:, 1:2], axis=0)).then_inc(landed[q], 16)


def project(nc, g, m, l):
    a = g.a
    with ExitStack() as ctx:
        sb = lambda n, s, dt=F32: ctx.enter_context(nc.sbuf_tensor(f"{n}_{l}", s, dt))
        sem = semaphores(nc, ctx, f"_proj{l}")
        psum = lambda n, s: ctx.enter_context(nc.psum_tensor(f"{n}_{l}", s, F32))
        w = sb("w_in", [P, KT, D_IN])
        if not l:
            zeros, zeros_set, y_zeroed = sb("zeros", [P, D]), sem("zeros_set"), sem("y_zeroed")
        hT = [sb(f"hT{i}", [P, KT, P]) for i in range(2)]
        xn = [sb(f"xn{i}", [P, D]) for i in range(2)]
        if l:
            yb = [sb(f"yb{i}", [P, D]) for i in range(2)]
            idx = [sb(f"idx{i}", [P, 2], I32) for i in range(2)]
            waited = sem("waited")
            g2 = sb("g2", [P, 2, D])
            ln2 = sb("ln2", [P, 2, D])
        x_norm, v_norm = Norm(sb, sem, "x_norm", D), Norm(sb, sem, "v_norm", GW)
        if l:
            c_norm = Norm(sb, sem, "c_norm", D)
        T = psum("turned", [P, KT, P])
        A, B, C, Dk = psum("bankA", [P, 512]), psum("bankB", [P, 512]), psum("bankC", [P, 4, P]), psum("bankD", [P, P])
        x_ld, g2c_ld = sem("x_ld"), sem("g2_ctx_ld")
        ug_ld, w_ld, vec_ld, zero = sem("ug_ld"), sem("w_ld"), sem("vec_ld"), sem("zeroed")
        xn_ready, turned, mod_a, mod_v = sem("xn_ready"), sem("x_turned"), sem("mod_act"), sem("mod_dve")
        a_done, b_done, c_done, d_done = sem("a_done"), sem("b_done"), sem("c_done"), sem("d_done")
        a_free, b_free, c_free, d_free = sem("a_free"), sem("b_free"), sem("c_free"), sem("d_free")
        v_step = sem("v_step")
        if l:
            landed = [sem(f"y_landed{i}") for i in range(2)]
            copied, used = sem("idx_copied"), sem("y_used")
        kv_only = lambda t: l > 0 and isinstance(t, int) and t >= LT
        stream = lambda t: 1 if isinstance(t, int) and t >= LT else 0
        LOOP = 3

        def tiles(eng, body, steps=None, per=0):
            with loop(nc, eng, 0, LOOP) as i:
                if steps:
                    steps.enter(i, per)
                for q in range(2):
                    body(i * 2 + q, q)
            if steps:
                steps.leave(LOOP)
            for t in range(2 * LOOP, NT):
                body(t, t % 2)

        with nc.Block() as block:
            @block.sync
            def _(sp):
                wl = a["w_in"][l].rearrange("(p k) n -> p k n", k=KT)

                def weights(lo, hi, s):
                    sp.dma_start(w[:, :, lo:hi], wl[:, :, lo:hi]).then_inc(s, 16)

                if l:
                    g2_of = lambda s: g.mods[l - 1, s:s + 1, 5 * D:6 * D].to_broadcast([P, D])
                    sp.dma_start(g2[:, 0, :], g2_of(0)).then_inc(vec_ld, 16)
                    for j, n in enumerate(("ln2_g", "ln2_b")):
                        sp.dma_start(ln2[:, j, :], a[n][l - 1:l, :].to_broadcast([P, D])).then_inc(vec_ld, 16)
                    sp.wait_ge(landed[0], 32)
                weights(C_U, D_IN, ug_ld)
                weights(C_F, C_Q, w_ld)
                weights(C_Q, C_U, w_ld)
                if l:
                    sp.dma_start(g2[:, 1, :], g2_of(1)).then_inc(g2c_ld, 16)
                else:
                    sp.dma_start(g.x[:, 2:LT, :], a["x"][0, 2 * P:, :].rearrange("(t p) d -> p t d", p=P)).then_inc(x_ld, 16)
                    sp.dma_start(g.x[:, LT:NT, :], a["ctx"][0].rearrange("(t p) d -> p t d", p=P)).then_inc(x_ld, 16)
                if not l:
                    sp.wait_ge(zeros_set, 1)
                    sp.dma_start(g.y[FEWEST * P:, :].rearrange("(b p) d -> p b d", p=P),
                                 across(zeros[:, :], NSLOTMAX + 1 - FEWEST)).then_inc(y_zeroed, 16)
                    sp.wait_ge(y_zeroed, 16)

            @block.gpsimd
            def _(pool):
                if not l:
                    nc.gpsimd.memset(zeros[:, :], 0.0).then_inc(zeros_set, 1)
                if l:
                    fetch = lambda t, q: gather_experts(nc, pool, g, t, q, idx, xn, yb, landed, copied, waited)
                    fetch(0, 0)
                    fetch(1, 1)
                for lo, hi in ((0, PAD), (PAD + SEQ, PL + PAD), (PW - PAD, PW)):
                    nc.gpsimd.memset(m.pT[:, :, lo:hi], 0.0).then_inc(zero, 1)
                for lo in (0, P + SEQ):
                    nc.gpsimd.memset(m.kT[:, lo:lo + P], 0.0).then_inc(zero, 1)
                for b in (0, LT + 1):
                    nc.gpsimd.memset(m.v[:, b, :], 0.0).then_inc(zero, 1)

                def step(t, q):
                    if not (isinstance(t, int) and t >= NT - 2):
                        if l:
                            pool.wait_ge(used, t + 1)
                            pool.wait_ge(turned, t + 1)
                            fetch(t + 2, q)
                            norm_power(nc, pool, g, c_norm, t + 2)
                        norm_power(nc, pool, g, x_norm, t + 2)
                    if not kv_only(t):
                        norm_power(nc, pool, g, v_norm, t)

                for t in range(2):
                    if l:
                        norm_power(nc, pool, g, c_norm, t)
                    norm_power(nc, pool, g, x_norm, t)
                tiles(pool, step)
                pool.wait_ge(zero, 7)

            @block.vector
            def _(v):
                s = Steps(v_step)

                def normalise(t, q):
                    if not l and not (isinstance(t, int) and t < 2):
                        v.wait_ge(x_ld, 32)
                    if l:
                        v.wait_ge(landed[q], (t - q) * 16 + 32)
                        if isinstance(t, int) and t == 0:
                            v.wait_ge(vec_ld, 48)
                        if stream(t):
                            v.wait_ge(g2c_ld, 16)
                        combine(nc, v, s, g, t, xn[q][:, :], yb[q][:, :], g2[:, stream(t), :], ln2[:, 0, :], ln2[:, 1, :],
                                c_norm, used, None).then_inc(s.sem, s.up())
                        v.wait_ge(s.sem, s.at())
                    x = g.x[:, bass.ds(t, 1), :].rearrange("p a d -> p (a d)")
                    rows_norm(nc, v, s, x, xn[q][:, :], x_norm, t).then_inc(xn_ready, 1)

                def modulate(t, q):
                    v.wait_ge(turned, t + 1)
                    for k in range(4, KT):
                        i = nc.vector.tensor_scalar(hT[q][:, k, :], T[:, k, :], g.cols[:, l, stream(t), 1, k:k + 1],
                                                    g.cols[:, l, stream(t), 0, k:k + 1], ALU.mult, ALU.add)
                    i.then_inc(mod_v, 1)

                def step(t, q):
                    last = isinstance(t, int) and t == NT - 1
                    if not last:
                        modulate(t + 1, 1 - q)
                    if not (isinstance(t, int) and t >= NT - 2):
                        normalise(t + 2, q)
                    v.wait_ge(c_done, t + 1)
                    kdst = (m.kT, P) if not stream(t) else (m.kcT, -LT * P)
                    pdst = PAD if not stream(t) else PL + PAD - LT * P
                    if kv_only(t):
                        nc.vector.tensor_copy(m.kcT[:, at_tile(t, P, -LT * P)], C[:, 2, :]).then_inc(c_free, 1)
                    else:
                        nc.vector.tensor_copy(m.qT[:, :, at_tile(t)], C[:, 0:2, :])
                        nc.vector.tensor_copy(kdst[0][:, at_tile(t, P, kdst[1])], C[:, 2, :])
                        nc.vector.tensor_copy(m.pT[:, 0, at_tile(t, P, pdst)], C[:, 3, :]).then_inc(c_free, 1)
                        v.wait_ge(d_done, t + 1)
                        nc.vector.tensor_copy(m.pT[:, 1, at_tile(t, P, pdst)], Dk[:, :]).then_inc(d_free, 1)
                        v.wait_ge(a_free, t + 2)
                        sg = m.sg[:, bass.ds(t, 1), :].rearrange("p a c -> p (a c)")
                        rows_norm(nc, v, s, sg, sg, v_norm, t).then_inc(s.sem, s.up())

                normalise(0, 0)
                modulate(0, 0)
                normalise(1, 1)
                nc.vector.engine_nop().then_inc(c_free, 1)
                nc.vector.engine_nop().then_inc(d_free, 1)
                tiles(v, step, s, 24 if l else 8)

            @block.scalar
            def _(act):
                def modulate(t, q):
                    act.wait_ge(turned, t + 1)
                    for k in range(4):
                        i = nc.scalar.activation(hT[q][:, k, :], T[:, k, :], ACT.Identity,
                                                 bias=g.cols[:, l, stream(t), 0, k:k + 1], scale=g.cols[:, l, stream(t), 1, k:k + 1])
                    i.then_inc(mod_a, 1)

                def step(t, q):
                    tile = lambda x: x[:, bass.ds(t, 1), :].rearrange("p a c -> p (a c)")
                    if not kv_only(t):
                        act.wait_ge(a_done, t + 1)
                        nc.scalar.activation(tile(m.u), A[:, 0:GW], ACT.Gelu)
                        nc.scalar.activation(tile(m.sg), A[:, GW:2 * GW], ACT.Gelu).then_inc(a_free, 1)
                    act.wait_ge(b_done, t + 1)
                    vb = 1 if not stream(t) else 2
                    if not kv_only(t):
                        nc.scalar.activation(tile(m.a), B[:, 0:GW], ACT.Copy)
                    nc.scalar.activation(m.v[:, bass.ds(t + vb, 1), :].rearrange("p a c -> p (a c)"), B[:, GW:GW + P], ACT.Copy).then_inc(b_free, 1)
                    if not (isinstance(t, int) and t == NT - 1):
                        modulate(t + 1, 1 - q)

                act.nop().then_inc(a_free, 1)
                act.nop().then_inc(b_free, 1)
                modulate(0, 0)
                tiles(act, step)

            @block.tensor
            def _(pe):
                def turn(t, q):
                    pe.wait_ge(xn_ready, t + 1)
                    for k in range(KT):
                        i = nc.tensor.transpose(T[:, k, :], xn[q][:, k::KT], g.k[:, K_ID:K_ID + P])
                    i.then_inc(turned, 1)

                def run(out, lhsT, rhs):
                    for k in range(KT):
                        i = nc.tensor.matmul(out, lhsT(k), rhs(k), start=k == 0, stop=k == KT - 1)
                    return i

                def step(t, q):
                    pe.wait_ge(mod_a, t + 1)
                    pe.wait_ge(mod_v, t + 1)
                    h = hT[q]
                    if not kv_only(t):
                        pe.wait_ge(a_free, t + 1)
                        pe.wait_ge(ug_ld, 16)
                        run(A[:, :], lambda k: h[:, k, :], lambda k: w[:, k, C_U:D_IN]).then_inc(a_done, 1)
                    pe.wait_ge(b_free, t + 1)
                    pe.wait_ge(w_ld, 32)
                    if not kv_only(t):
                        run(B[:, 0:GW], lambda k: h[:, k, :], lambda k: w[:, k, C_F:C_Q])
                    run(B[:, GW:GW + P], lambda k: h[:, k, :], lambda k: w[:, k, C_V:C_P]).then_inc(b_done, 1)
                    if not (isinstance(t, int) and t == NT - 1):
                        turn(t + 1, 1 - q)
                    pe.wait_ge(c_free, t + 1)
                    if not kv_only(t):
                        for j in range(2):
                            run(C[:, j, :], lambda k: w[:, k, C_Q + j * P:C_Q + (j + 1) * P], lambda k: h[:, k, :])
                    i = run(C[:, 2, :], lambda k: w[:, k, C_K:C_V], lambda k: h[:, k, :])
                    if not kv_only(t):
                        i = run(C[:, 3, :], lambda k: w[:, k, C_P:C_P + P], lambda k: h[:, k, :])
                    i.then_inc(c_done, 1)
                    if not kv_only(t):
                        pe.wait_ge(d_free, t + 1)
                        run(Dk[:, :], lambda k: w[:, k, C_P + P:C_U], lambda k: h[:, k, :]).then_inc(d_done, 1)

                turn(0, 0)
                tiles(pe, step)


def transform(nc, g, m, l):
    a = g.a
    ctx_out = l < DEPTH - 1
    R, RC = SEQ // P, CTX // P
    with ExitStack() as ctx:
        sb = lambda n, s, dt=F32: ctx.enter_context(nc.sbuf_tensor(f"{n}_{l}", s, dt))
        sem = semaphores(nc, ctx, f"_trans{l}")
        psum = lambda n, s: ctx.enter_context(nc.psum_tensor(f"{n}_{l}", s, F32))
        dft, dftc = sb("dft", [P, R, 4 * P]), sb("dft_ctx", [P, RC, 2 * P])
        rope = sb("rope", [P, 2, SEQ])
        wf = sb("w_fourier", [P, 2, GW])
        wc = sb("w_chan", [P, 2, 2, GW])
        wp = sb("w_pool", [P, 2, P])
        psc = sb("pool_scale", [P, 2])
        z = sb("z", [P, 8, GW])
        zt = sb("z_tmp", [P, 12, GW])
        zc = sb("z_ctx", [P, RC, GW])
        X = sb("spectrumT", [P, 2, 2, NT * P])
        pa, pb = sb("pool_a", [P, 2, PW]), sb("pool_b", [P, 2, PW])
        edge = sb("pool_edge", [P, 2, 2, 16])
        Dp = [psum(f"dft_ps{i}", [P, 512]) for i in range(4)]
        M = [psum(f"mix_ps{i}", [P, 512]) for i in range(4)]
        wf_in, dft_in, rope_in, pool_in, wpz = sem("wf_in"), sem("dft_in"), sem("rope_in"), sem("pool_in"), sem("wp_zero")
        v_step, z_done = sem("v_step"), sem("z_done")
        wc_mm, wc_done = sem("wc_mm"), sem("wc_done")
        dft_mm, dft_out = sem("dft_mm"), sem("dft_out")
        rot_mm, rot_free = sem("rot_mm"), sem("rot_free")
        cos_done = sem("cos_done")
        pooled, four_mm, four_out, pl_mm, pl_out = sem("pooled"), sem("four_mm"), sem("four_out"), sem("pool_mm"), sem("pool_out")
        PARTS = {0: (0,), 4: (1,), 2: (2, 3), 6: (2, 3), 1: (4, 5), 7: (4, 5), 3: (6, 7), 5: (6, 7)}
        jobs = [(0, k1, h) for k1 in range(R) for h in range(2)]
        if ctx_out:
            jobs += [(1, k1, h) for k1 in range(RC) for h in range(2)]
        spans = [(0, 512), (512, 512)] + ([(SEQ, CTX)] if ctx_out else [])
        RUNS = [(t, n) for t in range(3) for n in range(2)]

        def qk(t, n):
            return m.qT[:, t, n * 512:n * 512 + 512] if t < 2 else m.kT[:, P + n * 512:P + n * 512 + 512]

        with nc.Block() as block:
            @block.sync
            def _(sp):
                sp.dma_start(wf[:, :, :], a["w_fourier"][l].rearrange("(h p) n -> p h n", p=P)).then_inc(wf_in, 16)
                sp.dma_start(dft[:, :, :], a["dft"]).then_inc(dft_in, 16)
                sp.dma_start(dftc[:, :, :], a["dft_ctx"]).then_inc(dft_in, 16)
                sp.dma_start(rope[:, :, :], a["rope"]).then_inc(rope_in, 16)
                sp.dma_start(psc[:, :], a["pool_scale"][l]).then_inc(pool_in, 16)
                sp.wait_ge(wpz, 1)
                for w in range(4):
                    o = w % 2 * HD
                    sp.dma_start(wp[o:o + HD, w // 2, o:o + HD], a["w_pool"][l, w]).then_inc(pool_in, 16)

            @block.gpsimd
            def _(pool):
                nc.gpsimd.memset(wp[:, :, :], 0.0).then_inc(wpz, 1)
                pool.wait_ge(rope_in, 16)
                for i, (t, n) in enumerate(RUNS):
                    pool.wait_ge(rot_mm, i + 1)
                    nc.gpsimd.tensor_tensor(qk(t, n), qk(t, n), rope[:, 0, n * 512:n * 512 + 512], ALU.mult).then_inc(cos_done, 1)

            @block.vector
            def _(v):
                s = Steps(v_step)
                c8 = float(np.sqrt(0.5))
                xr = [m.a[:, r, :] for r in range(R)]
                T = [zt[:, i, :] for i in range(12)]
                Z = [z[:, i, :] for i in range(8)]

                def two(o, x, y, op):
                    nc.vector.tensor_tensor(o, x, y, op).then_inc(s.sem, s.up())

                for i in range(4):
                    j = (0, 2, 1, 3)[i]
                    two(T[2 * i], xr[j], xr[j + 4], ALU.add)
                    two(T[2 * i + 1], xr[j], xr[j + 4], ALU.subtract)
                v.wait_ge(s.sem, s.at())
                two(T[8], T[0], T[2], ALU.add)
                two(T[9], T[4], T[6], ALU.add)
                two(Z[2], T[0], T[2], ALU.subtract)
                two(Z[3], T[6], T[4], ALU.subtract)
                two(T[10], T[5], T[7], ALU.subtract)
                two(T[11], T[5], T[7], ALU.add)
                v.wait_ge(s.sem, s.at())
                two(Z[0], T[8], T[9], ALU.add)
                two(Z[1], T[8], T[9], ALU.subtract)
                for o, x, c, y, op in ((Z[4], T[10], c8, T[1], ALU.add), (Z[5], T[11], -c8, T[3], ALU.subtract),
                                       (Z[6], T[10], -c8, T[1], ALU.add), (Z[7], T[11], -c8, T[3], ALU.add)):
                    nc.vector.scalar_tensor_tensor(o, x, c, y, ALU.mult, op).then_inc(s.sem, s.up())
                v.wait_ge(s.sem, s.at())
                if ctx_out:
                    nc.vector.tensor_tensor(zc[:, 1, :], m.a[:, LT, :], m.a[:, LT + 1, :], ALU.subtract).then_inc(z_done, 1)
                    nc.vector.tensor_tensor(zc[:, 0, :], m.a[:, LT, :], m.a[:, LT + 1, :], ALU.add).then_inc(z_done, 1)
                else:
                    nc.vector.engine_nop().then_inc(z_done, 2)

                v.wait_ge(wc_mm, 1)
                nc.vector.tensor_copy(wc[:, :, :, :].rearrange("p h c n -> p (h c n)").rearrange("p (b n) -> p b n", b=2)[:, 0, :], M[0][:, :]).then_inc(wc_done, 1)
                nc.vector.tensor_copy(wc[:, :, :, :].rearrange("p h c n -> p (h c n)").rearrange("p (b n) -> p b n", b=2)[:, 1, :], M[1][:, :]).then_inc(wc_done, 1)

                p, A, B = m.pT, pa, pb
                streams = [(PAD, SEQ)] + ([(PL + PAD, CTX)] if ctx_out else [])

                def halves(o, x, lo, hi, sh, rows, t):
                    for base, n in streams:
                        b0, b1 = base - lo, base + n + hi
                        nc.vector.tensor_tensor(o[rows, t, b0:b1], x[rows, t, b0 - sh[0]:b1 - sh[0]], x[rows, t, b0 + sh[1]:b1 + sh[1]],
                                                ALU.add).then_inc(s.sem, s.up())
                every, upper = slice(0, P), slice(HD, P)
                for t in range(2):
                    halves(A, p, 7, 7, (1, 0), every, t)
                v.wait_ge(s.sem, s.at())
                halves(B, A, 6, 6, (1, 1), upper, 0)
                halves(B, A, 6, 6, (1, 1), every, 1)
                v.wait_ge(s.sem, s.at())
                halves(A, B, 4, 4, (2, 2), every, 1)
                v.wait_ge(s.sem, s.at())
                halves(B, A, 0, 0, (4, 4), upper, 1)
                v.wait_ge(s.sem, s.at())
                low = slice(0, HD)
                ends = [(0, PAD, 0), (0, PAD + SEQ - 8, 8)]
                if ctx_out:
                    ends += [(1, PL + PAD, 0), (1, PL + PAD + CTX - 8, 8)]
                for rows, src in ((low, A), (upper, B)):
                    for st, c0, e0 in ends:
                        nc.vector.tensor_tensor(edge[rows, st, :, e0:e0 + 8], src[rows, :, c0:c0 + 8],
                                                g.k[rows, K_EDGE:K_EDGE + 32].rearrange("p (t e) -> p t e", t=2)[:, :, e0:e0 + 8],
                                                ALU.mult).then_inc(s.sem, s.up())
                v.wait_ge(s.sem, s.at())
                for rows, src in ((low, A), (upper, B)):
                    for t in range(2):
                        for c0, n in streams:
                            nc.vector.scalar_tensor_tensor(A[rows, t, c0:c0 + n], src[rows, t, c0:c0 + n], g.k[rows, K_IW + t:K_IW + t + 1],
                                                           p[rows, t, c0:c0 + n], ALU.mult, ALU.subtract).then_inc(s.sem, s.up())
                v.wait_ge(s.sem, s.at())
                for n, (st, c0, e0) in enumerate(ends):
                    nc.vector.tensor_tensor(A[:, :, c0:c0 + 8], edge[:, st, :, e0:e0 + 8], p[:, :, c0:c0 + 8],
                                            ALU.subtract).then_inc(pooled, 1)

                v.wait_ge(rope_in, 16)
                for i, (t, n) in enumerate(RUNS):
                    v.wait_ge(rot_mm, i + 1)
                    if i:
                        v.wait_ge(s.sem, s.at())
                    r = M[2 + i % 2]
                    nc.vector.tensor_tensor(pb[:, 0, 0:512] if i % 2 else pb[:, 1, 0:512], r[:, :], rope[:, 1, n * 512:n * 512 + 512],
                                            ALU.mult).then_inc(rot_free, 1)
                    v.wait_ge(rot_free, i + 3)
                    v.wait_ge(cos_done, i + 1)
                    nc.vector.tensor_tensor(qk(t, n), qk(t, n), pb[:, 0, 0:512] if i % 2 else pb[:, 1, 0:512], ALU.add).then_inc(s.sem, s.up())

            @block.scalar
            def _(act):
                for i, (st, k1, h) in enumerate(jobs):
                    act.wait_ge(dft_mm, i + 1)
                    dst = X[:, h, :, k1:SEQ:R] if st == 0 else X[:, h, :, SEQ + k1:SEQ + CTX:RC]
                    nc.scalar.activation(dst, Dp[i % 4][:, 0:2 * P].rearrange("p (c n) -> p c n", c=2), ACT.Copy).then_inc(dft_out, 1)
                act.wait_ge(pool_in, 80)
                for i, (t, (c0, n)) in enumerate([(t, sp_) for t in range(2) for sp_ in spans]):
                    act.wait_ge(pl_mm, i + 1)
                    o = c0 + (PAD if c0 < SEQ else 3 * PAD)
                    nc.scalar.activation(m.pT[:, t, o:o + n], Dp[i % 4][:, 0:n], ACT.Copy, scale=psc[:, t:t + 1]).then_inc(pl_out, 1)
                for i, (h, (c0, n)) in enumerate([(h, sp_) for h in range(2) for sp_ in spans]):
                    act.wait_ge(four_mm, i + 1)
                    nc.scalar.activation(m.four[:, h, c0:c0 + n], M[i % 2][:, 0:n], ACT.Copy).then_inc(four_out, 1)

            @block.tensor
            def _(pe):
                pe.wait_ge(wf_in, 16)
                for h in range(2):
                    for c in range(2):
                        mm = nc.tensor.matmul(M[h][:, c * GW:(c + 1) * GW], g.k[:, (K_CD, K_SD)[c]:(K_CD, K_SD)[c] + P], wf[:, h, :],
                                              start=True, stop=True)
                mm.then_inc(wc_mm, 1)
                pe.nop().then_inc(rot_free, 2)

                def rotate(i):
                    t, n = RUNS[i]
                    pe.wait_ge(rot_free, i + 1)
                    nc.tensor.matmul(M[2 + i % 2][:, :], g.k[:, K_ROT:K_ROT + P], qk(t, n), start=True, stop=True).then_inc(rot_mm, 1)

                rotate(0)
                rotate(1)
                pe.wait_ge(dft_in, 32)
                pe.wait_ge(z_done, 2)
                for i, (st, k1, h) in enumerate(jobs):
                    if i >= 4:
                        pe.wait_ge(dft_out, i - 3)
                    o = Dp[i % 4][:, 0:2 * P]
                    if st:
                        mm = nc.tensor.matmul(o, zc[:, k1, h * P:(h + 1) * P], dftc[:, k1, :], start=True, stop=True)
                    else:
                        parts = PARTS[k1]
                        for j, zi in enumerate(parts):
                            mm = nc.tensor.matmul(o, z[:, zi, h * P:(h + 1) * P], dft[:, k1, 2 * P * j:2 * P * (j + 1)],
                                                  start=j == 0, stop=j == len(parts) - 1)
                    mm.then_inc(dft_mm, 1)
                for i in range(2, len(RUNS)):
                    rotate(i)
                pe.wait_ge(pooled, 4 if ctx_out else 2)
                pe.wait_ge(pool_in, 80)
                pe.wait_ge(dft_out, len(jobs))
                for i, (t, (c0, n)) in enumerate([(t, sp_) for t in range(2) for sp_ in spans]):
                    if i >= 4:
                        pe.wait_ge(pl_out, i - 3)
                    o = c0 + (PAD if c0 < SEQ else 3 * PAD)
                    nc.tensor.matmul(Dp[i % 4][:, 0:n], wp[:, t, :], pa[:, t, o:o + n], start=True, stop=True).then_inc(pl_mm, 1)
                pe.wait_ge(wc_done, 2)
                for i, (h, (c0, n)) in enumerate([(h, sp_) for h in range(2) for sp_ in spans]):
                    if i >= 2:
                        pe.wait_ge(four_out, i - 1)
                    for j in range(4):
                        mm = nc.tensor.matmul(M[i % 2][:, 0:n], wc[:, j // 2, j % 2, h * P:(h + 1) * P], X[:, j // 2, j % 2, c0:c0 + n],
                                              start=j == 0, stop=j == 3)
                    mm.then_inc(four_mm, 1)


PER_B = 44


def attend(nc, g, m, l):
    a = g.a
    N = NT if l < DEPTH - 1 else LT
    BW = 3 * P
    KW = BW + CTX
    with ExitStack() as ctx:
        sb = lambda n, s, dt=F32: ctx.enter_context(nc.sbuf_tensor(f"{n}_{l}", s, dt))
        sem = semaphores(nc, ctx, f"_att{l}")
        psum = lambda n, s: ctx.enter_context(nc.psum_tensor(f"{n}_{l}", s, F32))
        wo = sb("w_out", [P, KT, D])
        wr = sb("w_router", [P, KT, NR])
        ws = sb("w_sguT", [P, NH, P])
        bs, sink = sb("b_sgu", [P, NH]), sb("sink", [P, NH])
        vec = sb("mod2", [P, 3, D])
        ln1 = sb("ln1", [P, 2, D])
        qs = [sb(f"q_head{i}", [P, NH, P]) for i in range(2)]
        pr = [sb(f"probs{i}", [P, 2, KW]) for i in range(2)]
        pT = sb("probsT", [P, 2, KW // P, P])
        nm, sums, sd, se = sb("neg_max", [P, NH]), sb("sums", [P, 2, NH]), sb("sink_diff", [P, NH]), sb("sink_exp", [P, NH])
        mx, mx2, den = sb("max_local", [P, 2]), sb("max_ctx", [P, 2]), sb("denominator", [P, NH])
        os = sb("heads_tok", [P, 2, GW])
        ys = [sb(f"mixT{i}", [P, KT, P]) for i in range(2)]
        hb = [sb(f"h2_{i}", [P, D]) for i in range(2)]
        hT = sb("h2T", [P, KT, P])
        S = psum("scores", [P, 2, 512])
        SC = psum("scores_ctx", [P, 2, CTX])
        T = [psum(f"turn{i}", [P, 4, P]) for i in range(2)]
        O = psum("head_out", [P, 2, GW])
        Y = psum("proj", [P, 2, 512])
        R = O[:, 0, 0:NR]
        n1, n2 = Norm(sb, sem, "norm1", D), Norm(sb, sem, "norm2", D)
        e = Core()
        e.norm1_done, e.gained, e.x_ready, e.waited, e.sink_in = (
            sem(n) for n in ("norm1_done", "gained", "x_ready", "waited", "sink_in"))
        e.g1_in, e.ln1_in = sem("g1_in"), sem("ln1_in")
        e.scored, e.maxed, e.expd, e.pt_full, e.pt_free, e.pv_done, e.o_ready = (
            sem(n) for n in ("scored", "maxed", "expd", "pt_full", "pt_free", "pv_done", "o_ready"))
        e.o_turned, e.o_free, e.fp_ready, e.q_ready, e.y0_full, e.y1_full, e.y_used = (
            sem(n) for n in ("o_turned", "o_free", "fp_ready", "q_ready", "y0_full", "y1_full", "y_used"))
        e.norm2_done, e.scaled2, e.h2_ready, e.h2a_full, e.h2b_full, e.h2T_ready, e.r_full = (
            sem(n) for n in ("norm2_done", "scaled2", "h2_ready", "h2a_full", "h2b_full", "h2T_ready", "r_full"))
        e.r_used, e.v_step, e.w_in, e.vec_in, e.small_in, e.vec_free, e.one_added = (
            sem(n) for n in ("r_used", "v_step", "w_in", "vec_in", "small_in", "vec_free", "one_added"))
        stored = [sem(f"h2_stored{i}") for i in range(2)]
        is_ctx = lambda t: isinstance(t, int) and t >= LT
        FIRST, PAIRS = 3, 2

        def iterations(eng, body, steps=None, per=0):
            for t in range(FIRST):
                body(t, t % 2)
            with loop(nc, eng, 0, PAIRS) as i:
                if steps:
                    steps.enter(i, per)
                for j in range(2):
                    body(i * 2 + (FIRST + j), (FIRST + j) % 2)
            if steps:
                steps.leave(PAIRS)
            for t in range(FIRST + 2 * PAIRS, N + 2):
                body(t, t % 2)

        att = lambda t: not isinstance(t, int) or t < N
        prj = lambda t: not isinstance(t, int) or 1 <= t <= N
        rtr = lambda t: not isinstance(t, int) or t >= 2
        last = lambda t: isinstance(t, int) and t == N - 1
        known = lambda t, lo: not isinstance(t, int) or t >= lo

        with nc.Block() as block:
            @block.sync
            def _(sp):
                def vectors(s, which):
                    for j in which:
                        sp.dma_start(vec[:, j, :], g.mods[l, s:s + 1, (j + 2) * D:(j + 3) * D].to_broadcast([P, D])).then_inc(
                            e.g1_in if j == 0 else e.vec_in, 16)

                sp.dma_start(sink[:, :], a["attn_sink"][l:l + 1, :].to_broadcast([P, NH])).then_inc(e.sink_in, 16)
                sp.dma_start(bs[:, :], a["b_sgu"][l]).then_inc(e.small_in, 16)
                sp.dma_start(ws[:, :, :], a["w_sgu"][l]).then_inc(e.small_in, 16)
                vectors(0, (0, 1, 2))
                sp.dma_start(wr[:, :, 0:NG], a["w_router_group"][l].rearrange("(k p) n -> p k n", p=P)).then_inc(e.small_in, 16)
                sp.dma_start(wr[:, :, NG:NR], a["w_router_expert"][l].rearrange("(k p) g n -> p k (g n)", p=P)).then_inc(e.small_in, 16)
                sp.dma_start(wo[:, :, :], a["w_out"][l].rearrange("(k p) n -> p k n", p=P)).then_inc(e.w_in, 16)
                for j, n in enumerate(("ln1_g", "ln1_b")):
                    sp.dma_start(ln1[:, j, :], a[n][l:l + 1, :].to_broadcast([P, D])).then_inc(e.ln1_in, 16)

                def step(t, q):
                    if isinstance(t, int) and t == LT + 1 and N > LT:
                        sp.wait_ge(e.y_used, LT)
                        vectors(1, (0,))
                        sp.wait_ge(e.vec_free, 1)
                        vectors(1, (1, 2))
                    if rtr(t):
                        sp.wait_ge(e.h2_ready, t - 1)
                        sp.dma_start(g.h2[at_tile(t - 2), :], hb[q][:, :]).then_inc(stored[q], 16)

                iterations(sp, step)
                for i in range(2):
                    sp.wait_ge(stored[i], 16 * N // 2)

            @block.gpsimd
            def _(pool):

                def add_one(s):
                    pool.wait_ge(e.vec_in, 32 if s == 0 else 64)
                    nc.gpsimd.tensor_scalar(vec[:, 2, :], vec[:, 2, :], 1.0, None, ALU.add).then_inc(e.one_added, 1)
                    pool.wait_ge(e.one_added, s + 1)

                def step(t, q):
                    if rtr(t):
                        norm_power(nc, pool, g, n2, t - 2)
                        if not last(t - 2):
                            modulate_part(t - 1, 1 - q)
                    if att(t + 1):
                        attention_part(t + 1, 1 - q)
                    if prj(t):
                        if not known(t, 2):
                            pool.wait_ge(e.ln1_in, 32)
                        norm_power(nc, pool, g, n1, t - 1)
                        if not last(t - 1):
                            gain_part(t)

                def gain_part(t):
                    x = g.x[:, bass.ds(t - 1, 1), :].rearrange("p a d -> p (a d)")
                    pool.wait_ge(e.norm1_done, t)
                    take_wait(pool, e.waited)
                    nc.gpsimd.tensor_tensor(x, x, ln1[:, 0, :], ALU.mult).then_inc(e.gained, 1)
                    pool.wait_ge(e.gained, t)
                    take_wait(pool, e.waited)
                    nc.gpsimd.tensor_tensor(x, x, ln1[:, 1, :], ALU.add).then_inc(e.x_ready, 1)

                def attention_part(t, q):
                    if known(t, 2):
                        pool.wait_ge(e.scored, t * 2 - 2)
                    for kv in range(NKV):
                        own_rows = g.k[:, K_KV + kv:K_KV + kv + 1].unsqueeze(2).to_broadcast([P, 2, P])
                        i = nc.gpsimd.tensor_tensor(qs[q][:, 2 * kv:2 * kv + 2, :], m.qT[:, :, at_tile(t)], own_rows, ALU.mult)
                    i.then_inc(e.q_ready, 1)
                    if known(t, 2):
                        pool.wait_ge(e.y1_full, t - 1)
                    nc.gpsimd.tensor_copy(ys[q][:, 4:6, :], m.four[:, :, at_tile(t)])
                    o = PAD if not is_ctx(t) else 3 * PAD
                    nc.gpsimd.tensor_copy(ys[q][:, 6:8, :], m.pT[:, :, at_tile(t, P, o)]).then_inc(e.fp_ready, 1)

                def modulate_part(t, q):
                    if isinstance(t, int) and t == LT + 1:
                        add_one(1)
                    h = hb[1 - q]
                    pool.wait_ge(e.norm2_done, t)
                    nc.gpsimd.tensor_tensor(h[:, :], h[:, :], vec[:, 2, :], ALU.mult).then_inc(e.scaled2, 1)
                    pool.wait_ge(e.scaled2, t)
                    nc.gpsimd.tensor_tensor(h[:, :], h[:, :], vec[:, 1, :], ALU.add).then_inc(e.h2_ready, 1)
                    if isinstance(t, int) and t == LT:
                        pool.wait_ge(e.h2_ready, LT)
                        nc.gpsimd.engine_nop().then_inc(e.vec_free, 1)

                attention_part(0, 0)
                add_one(0)
                iterations(pool, step)

            @block.vector
            def _(v):
                s = Steps(e.v_step)
                small = lambda i: i.then_inc(s.sem, s.up())

                def maxima(t, pair):
                    v.wait_ge(e.scored, t * 2 + pair + 1)
                    h = slice(2 * pair, 2 * pair + 2)
                    if not is_ctx(t):
                        kind = 1 if not isinstance(t, int) else 0 if t == 0 else 2 if t == LT - 1 else 1
                        mask = g.k[:, K_MASK + kind * 2 * P:K_MASK + (kind + 1) * 2 * P].rearrange("p (s j) -> p s j", s=2)
                        for i in range(2):
                            own = S[:, i, 0:4 * P].rearrange("p (s w j) -> p s w j", s=2, w=2)[:, :, 0, :]
                            small(nc.vector.tensor_tensor(own, own, mask, ALU.add))
                        v.wait_ge(s.sem, s.at())
                        small(nc.vector.tensor_reduce(mx[:, :], S[:, :, 0:BW], AX, ALU.max))
                    if pair or known(t, 1):
                        v.wait_ge(e.maxed, t * 4 + pair * 2)
                    small(nc.vector.tensor_reduce(mx2[:, :], SC[:, :, :], AX, ALU.max))
                    v.wait_ge(s.sem, s.at())
                    if not is_ctx(t):
                        small(nc.vector.tensor_tensor(mx2[:, :], mx[:, :], mx2[:, :], ALU.max))
                        v.wait_ge(s.sem, s.at())
                    small(nc.vector.scalar_tensor_tensor(mx2[:, :], mx2[:, :], SCALE, sink[:, h], ALU.mult, ALU.max))
                    v.wait_ge(s.sem, s.at())
                    nc.vector.tensor_scalar(nm[:, h], mx2[:, :], -1.0, None, ALU.mult).then_inc(e.maxed, 1)
                    nc.vector.tensor_tensor(sd[:, h], sink[:, h], mx2[:, :], ALU.subtract).then_inc(e.maxed, 1)

                def heads(t, q):
                    if known(t, 1):
                        v.wait_ge(e.o_turned, t)
                    v.wait_ge(e.expd, t * 2 + 2)
                    small(nc.vector.tensor_tensor(den[:, :], sums[:, 1, :], se[:, :], ALU.add))
                    v.wait_ge(s.sem, s.at())
                    if not is_ctx(t):
                        small(nc.vector.tensor_tensor(den[:, :], den[:, :], sums[:, 0, :], ALU.add))
                        v.wait_ge(s.sem, s.at())
                    small(nc.vector.reciprocal(den[:, :], den[:, :]))
                    v.wait_ge(s.sem, s.at())
                    v.wait_ge(e.pv_done, t * 2 + 2)
                    if not known(t, 1):
                        v.wait_ge(e.small_in, 64)
                    b = over(bs[:, :], HD)
                    r4 = lambda x: x.rearrange("p (h c) -> p h c", h=NH)
                    small(nc.vector.tensor_tensor(r4(os[:, 1, :]), r4(O[:, 1, :]), b, ALU.add))
                    v.wait_ge(s.sem, s.at())
                    small(nc.vector.tensor_tensor(os[:, 1, :], os[:, 1, :], m.u[:, bass.ds(t, 1), :].rearrange("p a c -> p (a c)"), ALU.mult))
                    nc.vector.tensor_tensor(r4(os[:, 0, :]), r4(O[:, 0, :]), over(den[:, :], HD), ALU.mult).then_inc(e.o_ready, 1)

                def step(t, q):
                    if att(t):
                        maxima(t, 0)
                    if rtr(t):
                        x = g.x[:, bass.ds(t - 2, 1), :].rearrange("p a d -> p (a d)")
                        v.wait_ge(e.x_ready, t - 1)
                        rows_norm(nc, v, s, x, hb[q][:, :], n2, t - 2).then_inc(e.norm2_done, 1)
                        if last(t - 2):
                            h = hb[q][:, :]
                            v.wait_ge(e.norm2_done, N)
                            nc.vector.tensor_tensor(h, h, vec[:, 2, :], ALU.mult).then_inc(e.scaled2, 1)
                            v.wait_ge(e.scaled2, N)
                            nc.vector.tensor_tensor(h, h, vec[:, 1, :], ALU.add).then_inc(e.h2_ready, 1)
                    if att(t):
                        maxima(t, 1)
                    if rtr(t):
                        v.wait_ge(e.h2a_full, t - 1)
                        if known(t, 3):
                            v.wait_ge(e.r_full, t - 2)
                        nc.vector.tensor_copy(hT[:, 0:4, :], T[0][:, :, :]).then_inc(e.h2T_ready, 1)
                        v.wait_ge(e.h2b_full, t - 1)
                        nc.vector.tensor_copy(hT[:, 4:8, :], T[1][:, :, :]).then_inc(e.h2T_ready, 1)
                    if prj(t):
                        u, h = t - 1, hb[1 - q]
                        x = g.x[:, bass.ds(t - 1, 1), :].rearrange("p a d -> p (a d)")
                        if isinstance(t, int) and t in (1, LT + 1):
                            v.wait_ge(e.g1_in, 16 if t == 1 else 32)
                        if known(t, 3):
                            v.wait_ge(stored[1 - q], (t - 1 - (1 - q)) * 8)
                            v.wait_ge(e.h2b_full, t - 2)
                        v.wait_ge(e.y1_full, t)
                        nc.vector.tensor_tensor(h[:, :], Y[:, :, :].rearrange("p a n -> p (a n)"), vec[:, 0, :], ALU.mult).then_inc(e.y_used, 1)
                        v.wait_ge(e.y_used, t)
                        small(nc.vector.scalar_tensor_tensor(x, x, ALPHA, h[:, :], ALU.mult, ALU.add))
                        v.wait_ge(s.sem, s.at())
                        rows_norm(nc, v, s, x, x, n1, u).then_inc(e.norm1_done, 1)
                        if last(t - 1):
                            v.wait_ge(e.norm1_done, N)
                            nc.vector.tensor_tensor(x, x, ln1[:, 0, :], ALU.mult).then_inc(e.gained, 1)
                            v.wait_ge(e.gained, N)
                            nc.vector.tensor_tensor(x, x, ln1[:, 1, :], ALU.add).then_inc(e.x_ready, 1)
                    if att(t):
                        heads(t, q)

                v.wait_ge(e.sink_in, 16)
                iterations(v, step, s, PER_B)

            @block.scalar
            def _(act):
                def exps(t, pair):
                    act.wait_ge(e.maxed, t * 4 + pair * 2 + 2)
                    if known(t, 1):
                        act.wait_ge(e.pt_full, t * 6 + 3 * pair - 3)
                        if pair == 0:
                            act.wait_ge(e.o_ready, t)
                    for i in range(2):
                        h = 2 * pair + i
                        if not is_ctx(t):
                            nc.scalar.activation(pr[pair][:, i, 0:BW], S[:, i, 0:BW], ACT.Exp, bias=nm[:, h:h + 1], scale=SCALE,
                                                 accum_out=sums[:, 0, h:h + 1])
                        nc.scalar.activation(pr[pair][:, i, BW:KW], SC[:, i, :], ACT.Exp, bias=nm[:, h:h + 1], scale=SCALE,
                                             accum_out=sums[:, 1, h:h + 1])
                    nc.scalar.activation(se[:, 2 * pair:2 * pair + 2], sd[:, 2 * pair:2 * pair + 2], ACT.Exp).then_inc(e.expd, 1)

                def copy_turned(t, pair):
                    flat = pT[:, :, :, :].rearrange("p a j n -> p (a j) n")
                    if pair or known(t, 1):
                        act.wait_ge(e.pv_done, t * 2 + pair)
                    if is_ctx(t):
                        act.wait_ge(e.pt_full, t * 6 + pair * 3 + 3)
                        nc.scalar.activation(pT[:, :, 3:5, :], T[1 - pair][:, :, :].rearrange("p (a j) n -> p a j n", a=2),
                                             ACT.Copy).then_inc(e.pt_free, 3)
                        return
                    for j in range(3):
                        lo, hi = 4 * j, min(4 * j + 4, 10)
                        act.wait_ge(e.pt_full, t * 6 + pair * 3 + j + 1)
                        nc.scalar.activation(flat[:, lo:hi, :], T[(1 + pair + j) % 2][:, 0:hi - lo, :], ACT.Copy).then_inc(e.pt_free, 1)

                def step(t, q):
                    if prj(t):
                        act.wait_ge(e.o_turned, t)
                        if known(t, 3):
                            act.wait_ge(e.y1_full, t - 2)
                        nc.scalar.activation(ys[1 - q][:, 0:4, :], T[0][:, :, :], ACT.Copy).then_inc(e.o_free, 1)
                    if att(t):
                        exps(t, 0)
                        copy_turned(t, 0)
                        exps(t, 1)
                    if rtr(t):
                        act.wait_ge(e.r_full, t - 1)
                        nc.scalar.activation(g.logits[:, bass.ds(t - 2, 1), :].rearrange("p a n -> p (a n)"), R, ACT.Copy).then_inc(e.r_used, 1)
                    if att(t):
                        copy_turned(t, 1)

                iterations(act, step)

            @block.tensor
            def _(pe):
                ident = g.k[:, K_ID:K_ID + P]

                def scores(t, q, pair):
                    if pair or known(t, 1):
                        pe.wait_ge(e.expd, t * 2 + pair)
                    for i in range(2):
                        qh = qs[q][:, 2 * pair + i, :]
                        if not is_ctx(t):
                            keys = m.kT[:, bass.ds(t * P, BW)] if not isinstance(t, int) else m.kT[:, t * P:t * P + BW]
                            nc.tensor.matmul(S[:, i, 0:BW], qh, keys, start=True, stop=True)
                        mm = nc.tensor.matmul(SC[:, i, :], qh, m.kcT[:, :], start=True, stop=True)
                    mm.then_inc(e.scored, 1)

                def turn_probs(t, pair):
                    pe.wait_ge(e.expd, t * 2 + pair + 1)
                    flat = pr[pair][:, :, :].rearrange("p a n -> p (a n)")
                    blocks = [[0, 1, 2, 3], [4, 5, 6, 7], [8, 9]] if not is_ctx(t) else [[3, 4, 8, 9]]
                    for j, group in enumerate(blocks):
                        if pair == 0 and j == 0:
                            if known(t, 1):
                                pe.wait_ge(e.pt_free, t * 6)
                        elif pair == 0 and j == 1:
                            if known(t, 1):
                                pe.wait_ge(e.o_free, t)
                        elif pair == 1 and j < 2 and rtr(t):
                            pe.wait_ge(e.h2T_ready, t * 2 - 3 + j)
                        else:
                            pe.wait_ge(e.pt_free, t * 6 + 3 * pair + j - 1)
                        for n, b in enumerate(group):
                            tr = nc.tensor.transpose(T[(1 + pair + j) % 2][:, n, :], flat[:, b * P:(b + 1) * P], ident)
                        tr.then_inc(e.pt_full, 3 if is_ctx(t) else 1)

                def values(t, pair):
                    pe.wait_ge(e.pt_free, t * 6 + 3 * pair + 3)
                    if pair == 0 and known(t, 1):
                        pe.wait_ge(e.o_ready, t)
                    if pair == 0 and rtr(t):
                        pe.wait_ge(e.r_used, t - 1)
                    for i in range(2):
                        js = range(5) if not is_ctx(t) else (3, 4)
                        for j in js:
                            block = t + j if j < 3 else LT + 2 + j - 3
                            v = m.v[:, bass.ds(block, 1), :].rearrange("p a c -> p (a c)")[:, pair * HD:(pair + 1) * HD]
                            h = 2 * pair + i
                            mm = nc.tensor.matmul(O[:, 0, h * HD:(h + 1) * HD], pT[:, i, j, :], v, start=j == js[0], stop=j == 4)
                    mm.then_inc(e.pv_done, 1)

                def gate(t):
                    sg = m.sg[:, bass.ds(t, 1), :].rearrange("p a c -> p (a c)")
                    for h in range(NH):
                        nc.tensor.matmul(O[:, 1, h * HD:(h + 1) * HD], ws[:, h, :], sg[:, h * HD:(h + 1) * HD], start=True, stop=True)

                def project_half(t, q, half):
                    if half == 0:
                        pe.wait_ge(e.o_free, t)
                        pe.wait_ge(e.fp_ready, t)
                        if known(t, 2):
                            pe.wait_ge(e.y_used, t - 1)
                    for j, k in enumerate((2, 3, 6, 7, 0, 1, 4, 5)):
                        mm = nc.tensor.matmul(Y[:, half, :], ys[1 - q][:, j, :], wo[:, k, half * 512:(half + 1) * 512], start=j == 0, stop=j == KT - 1)
                    mm.then_inc((e.y0_full, e.y1_full)[half], 1)

                def step(t, q):
                    if att(t):
                        pe.wait_ge(e.q_ready, t + 1)
                        scores(t, q, 0)
                    if prj(t):
                        pe.wait_ge(e.o_ready, t)
                        pe.wait_ge(e.pt_free, t * 6)
                        for j in range(4):
                            tr = nc.tensor.transpose(T[0][:, j, :], os[:, j // 2, j % 2 * P:(j % 2 + 1) * P], ident)
                        tr.then_inc(e.o_turned, 1)
                    if prj(t):
                        if not known(t, 2):
                            pe.wait_ge(e.w_in, 16)
                        project_half(t, q, 0)
                    if att(t):
                        turn_probs(t, 0)
                        scores(t, q, 1)
                    if rtr(t):
                        pe.wait_ge(e.h2_ready, t - 1)
                        if att(t):
                            pe.wait_ge(e.pt_free, t * 6 + 3)
                        elif prj(t):
                            pe.wait_ge(e.o_free, t)
                        for j in range(4):
                            tr = nc.tensor.transpose(T[0][:, j, :], hb[q][:, j * P:(j + 1) * P], ident)
                        tr.then_inc(e.h2a_full, 1)
                        for j in range(4):
                            tr = nc.tensor.transpose(T[1][:, j, :], hb[q][:, (j + 4) * P:(j + 5) * P], ident)
                        tr.then_inc(e.h2b_full, 1)
                    if prj(t):
                        project_half(t, q, 1)
                    if rtr(t):
                        pe.wait_ge(e.h2T_ready, t * 2 - 2)
                        pe.wait_ge(e.o_ready, t if att(t) else N)
                        if known(t, 3):
                            pe.wait_ge(e.r_used, t - 2)
                        for k in range(KT):
                            mm = nc.tensor.matmul(R, hT[:, k, :], wr[:, k, :], start=k == 0, stop=k == KT - 1)
                        mm.then_inc(e.r_full, 1)
                    if att(t):
                        if not known(t, 1):
                            pe.wait_ge(e.small_in, 64)
                        values(t, 0)
                        turn_probs(t, 1)
                        gate(t)
                        values(t, 1)

                iterations(pe, step)


def route_and_experts(nc, g, l):
    a = g.a
    N = NT if l < DEPTH - 1 else LT
    NB_MAX = N * P * 2 // P + NE
    NB_MIN = N * P * 2 // P
    CB = N * P // P
    with ExitStack() as ctx:
        sb = lambda n, s, dt=F32: ctx.enter_context(nc.sbuf_tensor(f"{n}_{l}", s, dt))
        sem = semaphores(nc, ctx, f"_moe{l}")
        psum = lambda n, s: ctx.enter_context(nc.psum_tensor(f"{n}_{l}", s, F32))
        G, E = g.logits[:, 0:N, 0:NG], g.logits[:, 0:N, NG:NR].rearrange("p t (g e) -> p t g e", g=NG)
        gtop, gdiff, gexp, gsum = sb("group_top", [P, N]), sb("group_diff", [P, N, NG]), sb("group_exp", [P, N, NG]), sb("group_sum", [P, N])
        gtie, goh = sb("group_tie", [P, N]), sb("group_hot", [P, N, NG])
        masked, sel = sb("masked", [P, N, NG, EPG]), sb("fine_logits", [P, N, EPG])
        top = [sb(f"fine_top{k}", [P, N]) for k in range(2)]
        tie, eoh = sb("fine_tie", [P, N]), [sb(f"fine_hot{k}", [P, N, EPG]) for k in range(2)]
        ediff, eexp, esum = sb("fine_diff", [P, N]), sb("fine_exp", [P, N]), sb("fine_sum", [P, N])
        hot = [sb(f"expert_hot{k}", [P, N, NG, EPG]) for k in range(2)]
        both = sb("expert_both", [P, N, NE])
        tot = sb("running_total", [P, N, NE])
        cmp_n, nb = sb("count_cmp", [P, NE, CB]), sb("expert_blocks", [P, NE])
        end = [sb(f"block_end{i}", [P, NE]) for i in range(2)]
        start = sb("block_start", [P, NE])
        diag, end_col, cmp_e = sb("end_diag", [NE, NE]), sb("end_col", [NE, 1]), sb("end_cmp", [NE, NBT])
        cmp_c = sb("pair_cmp", [1, 2, NBT])
        half = sb("half_blocks", [1, 2])
        tab_f, tab = sb("table_f", [1, NBT + 2]), sb("table", [1, NBT + 2], I32)
        slot, posf = sb("slot_all", [P, N, NE]), sb("slot_f", [P, N, 2])
        place = [sb(f"slot_{n}", [P, N, 2], I32) for n in ("block", "row")]
        place_f = [sb(f"slot_{n}_f", [P, N, 2]) for n in ("block", "row")]
        ids_f = sb("token_ids_f", [P, N])
        blk_hot, row_hot = sb("block_hot", [P, N, 2, NBT]), sb("row_hot", [P, N, 2, P])
        tok = sb("slot_token", [P, NBT], I32)
        waited = sem("waited")
        wg, wu, wd = ([sb(f"{n}{i}", [P, KT, DE] if n != "w_down" else [P, JT, D]) for i in range(2)] for n in ("w_gate", "w_up", "w_down"))
        idx = [sb(f"rows_idx{i}", [P, 1], I32) for i in range(2)]
        xg = [sb(f"rows{i}", [P, D]) for i in range(2)]
        xT = sb("rowsT", [P, KT, P])
        silu, hid = sb("silu", [P, 2, P]), sb("hidT", [P, JT, P])
        yo = [sb(f"y_out{i}", [P, D]) for i in range(2)]
        T = psum("rows_turned", [P, KT, P])
        H = [psum(f"gate_up{i}", [P, 4, P]) for i in range(2)]
        Y = psum("down", [P, 2, 512])
        tok_ps, tab_ps = H[0][:, 0, 0:NBT], H[1][0:1, 0, 0:NBT]
        before, total = psum("tokens_before", [P, N * NE]), psum("tile_total", [P, N * NE])
        v_step, exp_in, exp_out, hot_ready, counted, prefixed = sem("v_step"), sem("exp_in"), sem("exp_out"), sem("hot_ready"), sem("counted"), sem("prefixed")
        cmp_ready, blocks_counted = sem("cmp_ready"), sem("blocks_counted")
        table_ready, slots_hot, slots_summed, slots_ready = (
            sem(n) for n in ("table_ready", "slots_hot", "slots_summed", "slots_ready"))
        g_in, u_in, d_in = ([sem(f"{n}_in{i}") for i in range(2)] for n in ("gate", "up", "down"))
        copied, rows_in = sem("idx_copied"), [sem(f"rows_in{i}") for i in range(2)]
        turned, xT_ready = sem("rows_turned"), sem("xT_ready")
        h_full, silu_done, hid_done = sem("h_full"), sem("silu_done"), sem("hid_done")
        y_full, y_done, stored = sem("y_full"), sem("y_done"), [sem(f"y_stored{i}") for i in range(2)]

        def blocks(eng, body):
            eng.wait_ge(table_ready, 1)
            full = eng.value_load(tab[0:1, NBT:NBT + 1], min_val=NB_MIN // 2, max_val=NB_MAX // 2)
            begun = eng.value_load(tab[0:1, NBT + 1:NBT + 2], min_val=NB_MIN // 2, max_val=(NB_MAX + 1) // 2)
            with loop(nc, eng, 0, full) as i:
                for q in range(2):
                    body(i, q)
            with eng.If_lt(eng.to_reg(full), eng.to_reg(begun)):
                body(full, 0)
            return full, begun

        with nc.Block() as block:
            @block.sync
            def _(sp):
                def weights(i, q):
                    b = i * 2 + q
                    e = sp.value_load(tab[0:1, bass.ds(b, 1)], min_val=0, max_val=NE - 1)
                    sp.wait_ge(h_full, b * 4 + 4)
                    for w, n, s in ((wg, "w_exp_gate", g_in), (wu, "w_exp_up", u_in)):
                        src = a[n][l][bass.ds(e, 1)].rearrange("a (p k) n -> p (a k) n", k=KT)
                        sp.dma_start(w[q][:, :, :], src).then_inc(s[q], 16)
                    if q == 0:
                        sp.wait_ge(rows_in[0], 16)
                    sp.wait_ge(y_full, b * 2 + 2)
                    src = a["w_exp_down"][l][bass.ds(e, 1)].rearrange("a (j p) n -> p (a j) n", p=P)
                    sp.dma_start(wd[q][:, :, :], src).then_inc(d_in[q], 16)

                blocks(sp, weights)

            @block.gpsimd
            def _(pool):
                pool.wait_ge(slots_ready, 1)

                def fetch(b, i, q):
                    nc.gpsimd.tensor_copy(idx[q][:, :], tok[:, bass.ds(b, 1)]).then_inc(copied, 1)
                    pool.wait_ge(copied, b + 1)
                    take_wait(pool, waited)
                    pool.indirect_dma_start(xg[q][:, :], None, g.h2[:, :],
                                            bass.IndirectOffsetOnAxis(ap=idx[q][:, 0:1], axis=0)).then_inc(rows_in[q], 16)

                def ahead(i, q):
                    pool.wait_ge(turned, i * 2 + q + 1)
                    fetch(i * 2 + q + 2, i + 1, q)

                fetch(0, 0, 0)
                fetch(1, 0, 1)
                full, begun = blocks(pool, ahead)
                pool.wait_ge(rows_in[0], begun * 16 + 16)
                pool.wait_ge(rows_in[1], full * 16 + 16)
                pool.wait_ge(stored[0], begun * 16 + 16)
                pool.wait_ge(stored[1], full * 16 + 16)

            @block.vector
            def _(v):
                s = Steps(v_step)
                step = lambda i: i.then_inc(s.sem, s.up())
                done = lambda: v.wait_ge(s.sem, s.at())
                tt, red, sts = nc.vector.tensor_tensor, nc.vector.tensor_reduce, nc.vector.scalar_tensor_tensor
                weight = lambda c, n: across(g.k[:, c:c + n], N)
                step(nc.vector.tensor_copy(ids_f[:, :], g.ids[:, 0:N]))
                step(red(gtop[:, :], G, AX, ALU.max))
                done()
                step(tt(gdiff[:, :, :], G, over(gtop[:, :], NG), ALU.subtract))
                done()
                nc.vector.engine_nop().then_inc(exp_in, 1)
                step(tt(goh[:, :, :], G, over(gtop[:, :], NG), ALU.is_equal))
                done()
                step(tt(goh[:, :, :], goh[:, :, :], weight(K_GW, NG), ALU.mult))
                done()
                step(red(gtie[:, :], goh[:, :, :], AX, ALU.max))
                done()
                step(tt(goh[:, :, :], goh[:, :, :], over(gtie[:, :], NG), ALU.is_equal))
                done()
                step(tt(masked[:, :, :, :], E, over(goh[:, :, :], EPG), ALU.mult))
                done()
                step(red(sel[:, :, :], masked[:, :, :, :].rearrange("p t g e -> p t e g"), AX, ALU.add))
                done()
                for k in range(2):
                    step(red(top[k][:, :], sel[:, :, :], AX, ALU.max))
                    done()
                    step(tt(eoh[k][:, :, :], sel[:, :, :], over(top[k][:, :], EPG), ALU.is_equal))
                    done()
                    step(tt(eoh[k][:, :, :], eoh[k][:, :, :], weight(K_EW, EPG), ALU.mult))
                    done()
                    step(red(tie[:, :], eoh[k][:, :, :], AX, ALU.max))
                    done()
                    step(tt(eoh[k][:, :, :], eoh[k][:, :, :], over(tie[:, :], EPG), ALU.is_equal))
                    done()
                    for j in range(NG):
                        step(tt(hot[k][:, :, j, :], over(goh[:, :, j], EPG), eoh[k][:, :, :], ALU.mult))
                    if k == 0:
                        step(sts(sel[:, :, :], eoh[0][:, :, :], -1e38, sel[:, :, :], ALU.mult, ALU.add))
                    done()
                flat = [h[:, :, :, :].rearrange("p t g e -> p t (g e)") for h in hot]
                tt(both[:, :, :], flat[0], flat[1], ALU.add).then_inc(hot_ready, 1)
                step(tt(ediff[:, :], top[1][:, :], top[0][:, :], ALU.subtract))
                done()
                nc.vector.engine_nop().then_inc(exp_in, 1)
                r = lambda x: x[:, :].rearrange("p (t e) -> p t e", t=N)
                v.wait_ge(counted, 1)
                step(nc.vector.tensor_copy(tot[:, :, :], r(total)))
                done()
                for t in range(1, N):
                    step(tt(tot[:, t, :], tot[:, t, :], tot[:, t - 1, :], ALU.add))
                    done()
                step(sts(cmp_n[:, :, :], across(g.k[:, K_IOTA:K_IOTA + CB], NE), float(P), over(tot[:, N - 1, :], CB), ALU.mult, ALU.is_lt))
                done()
                step(red(nb[:, :], cmp_n[:, :, :], AX, ALU.add))
                done()
                src = nb
                for i in range(5):
                    sh, dst = 1 << i, end[i % 2]
                    step(nc.vector.tensor_copy(dst[:, 0:sh], src[:, 0:sh]))
                    step(tt(dst[:, sh:NE], src[:, sh:NE], src[:, 0:NE - sh], ALU.add))
                    done()
                    src = dst
                step(tt(start[:, :], src[:, :], nb[:, :], ALU.subtract))
                step(tt(diag[:, :], src[0:NE, :], g.k[0:NE, K_ID:K_ID + NE], ALU.mult))
                step(nc.vector.tensor_scalar(half[:, 1:2], src[0:1, NE - 1:NE], 0.5, None, ALU.mult))
                step(nc.vector.tensor_scalar(half[:, 0:1], src[0:1, NE - 1:NE], 0.5, -0.5, ALU.mult, ALU.add))
                done()
                step(red(end_col[:, :], diag[:, :], AX, ALU.add))
                done()
                tt(cmp_e[:, :], end_col[:, 0:1].to_broadcast([NE, NBT]), g.k[0:NE, K_IOTA:K_IOTA + NBT], ALU.is_le).then_inc(cmp_ready, 1)
                step(tt(cmp_c[:, :, :], across(g.k[0:1, K_IOTA:K_IOTA + NBT], 2), over(half[:, :], NBT), ALU.is_lt))
                done()
                step(red(tab_f[:, NBT:NBT + 2], cmp_c[:, :, :], AX, ALU.add))
                v.wait_ge(blocks_counted, 1)
                step(nc.vector.tensor_scalar(tab_f[:, 0:NBT], tab_ps, float(NE - 1), None, ALU.min))
                done()
                nc.vector.tensor_copy(tab[:, :], tab_f[:, :]).then_inc(table_ready, 1)
                v.wait_ge(prefixed, 1)
                step(nc.vector.tensor_copy(slot[:, 0, :], r(before)[:, 0, :]))
                step(tt(slot[:, 1:N, :], r(before)[:, 1:N, :], tot[:, 0:N - 1, :], ALU.add))
                done()
                step(sts(slot[:, :, :], across(start[:, :], N), float(P), slot[:, :, :], ALU.mult, ALU.add))
                done()
                for k in range(2):
                    step(tt(flat[k], flat[k], slot[:, :, :], ALU.mult))
                done()
                for k in range(2):
                    step(red(posf[:, :, k], flat[k], AX, ALU.add))
                done()
                step(nc.vector.tensor_copy(g.pos[:, 0:N, :], posf[:, :, :]))
                done()
                step(nc.vector.tensor_scalar(place[0][:, :, :], g.pos[:, 0:N, :], 7, None, ALU.arith_shift_right))
                step(nc.vector.tensor_scalar(place[1][:, :, :], g.pos[:, 0:N, :], P - 1, None, ALU.bitwise_and))
                done()
                for i in range(2):
                    step(nc.vector.tensor_copy(place_f[i][:, :, :], place[i][:, :, :]))
                done()
                iota = lambda n: g.k[:, K_IOTA:K_IOTA + n].unsqueeze(1).unsqueeze(1).to_broadcast([P, N, 2, n])
                step(tt(blk_hot[:, :, :, :], iota(NBT), over(place_f[0][:, :, :], NBT), ALU.is_equal))
                tt(row_hot[:, :, :, :], iota(P), over(place_f[1][:, :, :], P), ALU.is_equal).then_inc(slots_hot, 1)
                done()
                tt(blk_hot[:, :, :, :], blk_hot[:, :, :, :], ids_f[:, :].unsqueeze(2).unsqueeze(2).to_broadcast([P, N, 2, NBT]),
                   ALU.mult).then_inc(slots_hot, 1)
                v.wait_ge(slots_summed, 1)
                nc.vector.tensor_copy(tok[:, :], tok_ps).then_inc(slots_ready, 1)
                v.wait_ge(exp_out, 2)
                step(red(gsum[:, :], gexp[:, :, :], AX, ALU.add))
                step(nc.vector.tensor_scalar(esum[:, :], eexp[:, :], 1.0, None, ALU.add))
                done()
                step(tt(gsum[:, :], gsum[:, :], esum[:, :], ALU.mult))
                done()
                step(nc.vector.reciprocal(g.gate[:, 0:N, 0], gsum[:, :]))
                done()
                step(tt(g.gate[:, 0:N, 1], g.gate[:, 0:N, 0], eexp[:, :], ALU.mult))
                done()

                def turn_copy(b):
                    v.wait_ge(turned, b + 1)
                    for h in range(2):
                        i = nc.vector.tensor_copy(xT[:, 4 * h:4 * h + 4, :], T[:, 4 * h:4 * h + 4, :])
                    i.then_inc(xT_ready, 1)

                nc.vector.engine_nop().then_inc(hid_done, 2)

                def products(i, q):
                    b = i * 2 + q
                    for j in range(JT):
                        v.wait_ge(silu_done, b * 4 + j + 1)
                        nc.vector.tensor_tensor(hid[:, j, :], silu[:, j % 2, :], H[j % 2][:, 1, :], ALU.mult).then_inc(hid_done, 1)
                    turn_copy(b + 1)

                turn_copy(0)
                blocks(v, products)

            @block.scalar
            def _(act):
                act.wait_ge(exp_in, 1)
                nc.scalar.activation(gexp[:, :, :], gdiff[:, :, :], ACT.Exp).then_inc(exp_out, 1)
                act.wait_ge(exp_in, 2)
                nc.scalar.activation(eexp[:, :], ediff[:, :], ACT.Exp).then_inc(exp_out, 1)
                for q in range(2):
                    act.nop().then_inc(stored[q], 16)

                def outputs(i, q):
                    b = i * 2 + q
                    for j in range(JT):
                        act.wait_ge(h_full, b * 4 + j + 9)
                        nc.scalar.activation(silu[:, j % 2, :], H[j % 2][:, 0, :], ACT.Silu).then_inc(silu_done, 1)
                    act.wait_ge(stored[q], i * 16 + 16)
                    for h in range(2):
                        act.wait_ge(y_full, b * 2 + h + 5)
                        nc.scalar.activation(yo[q][:, h * 512:(h + 1) * 512], Y[:, h, :], ACT.Copy).then_inc(y_done, 1)
                    act.wait_ge(y_done, b * 2 + 4)
                    act.dma_start(g.y[at_tile(b), :], yo[q][:, :]).then_inc(stored[q], 16)

                blocks(act, outputs)

            @block.tensor
            def _(pe):
                pe.nop().then_inc(h_full, 8)
                pe.nop().then_inc(y_full, 4)
                pe.nop().then_inc(y_done, 2)
                pe.wait_ge(hot_ready, 1)
                m = both[:, :, :].rearrange("p t e -> p (t e)")
                nc.tensor.matmul(total[:, :], g.k[:, K_ONE:K_ONE + P], m, start=True, stop=True).then_inc(counted, 1)
                nc.tensor.matmul(before[:, :], g.k[:, K_TRI:K_TRI + P], m, start=True, stop=True).then_inc(prefixed, 1)
                pe.wait_ge(cmp_ready, 1)
                nc.tensor.matmul(tab_ps, g.k[0:NE, K_ONE:K_ONE + 1], cmp_e[:, :], start=True, stop=True).then_inc(blocks_counted, 1)
                pe.wait_ge(slots_hot, 2)
                for i in range(2 * N):
                    mm = nc.tensor.matmul(tok_ps, row_hot[:, i // 2, i % 2, :], blk_hot[:, i // 2, i % 2, :], start=i == 0, stop=i == 2 * N - 1)
                mm.then_inc(slots_summed, 1)
                pe.wait_ge(slots_ready, 1)

                def turn(b, i, q):
                    pe.wait_ge(rows_in[q], i * 16 + 16)
                    for k in range(KT):
                        tr = nc.tensor.transpose(T[:, k, :], xg[q][:, k::KT], g.k[:, K_ID:K_ID + P])
                    tr.then_inc(turned, 1)

                def expert(i, q):
                    b = i * 2 + q
                    pe.wait_ge(xT_ready, b + 1)
                    pe.wait_ge(g_in[q], i * 16 + 16)
                    for j in range(JT):
                        pe.wait_ge(hid_done, b * 4 + j + 1)
                        for w, o in ((wg, 0), (wu, 1)):
                            if j == 0 and o == 1:
                                pe.wait_ge(u_in[q], i * 16 + 16)
                            for k in range(KT):
                                mm = nc.tensor.matmul(H[j % 2][:, o, :], w[q][:, k, j * P:(j + 1) * P], xT[:, k, :], start=k == 0, stop=k == KT - 1)
                        mm.then_inc(h_full, 1)
                    turn(b + 1, i + q, 1 - q)
                    pe.wait_ge(d_in[q], i * 16 + 16)
                    pe.wait_ge(hid_done, b * 4 + 6)
                    for h in range(2):
                        pe.wait_ge(y_done, b * 2 + h + 1)
                        for j in range(JT):
                            mm = nc.tensor.matmul(Y[:, h, :], hid[:, j, :], wd[q][:, j, h * 512:(h + 1) * 512], start=j == 0, stop=j == JT - 1)
                        mm.then_inc(y_full, 1)

                turn(0, 0, 0)
                blocks(pe, expert)


def finish(nc, g):
    l, BUF = DEPTH - 1, 4
    with ExitStack() as ctx:
        sb = lambda n, s, dt=F32: ctx.enter_context(nc.sbuf_tensor(f"{n}_end", s, dt))
        sem = semaphores(nc, ctx, "_end")
        ya, yb = ([sb(f"y{c}{i}", [P, D]) for i in range(BUF)] for c in "ab")
        idx = [sb(f"idx{i}", [P, 2], I32) for i in range(BUF)]
        g2, ln2 = sb("g2", [P, D]), sb("ln2", [P, 2, D])
        norm = Norm(sb, sem, "c_norm", D)
        mean = [sb(f"minus_mean{i}", [P, 1]) for i in range(2)]
        rstd = [sb(f"deviation{i}", [P, 1]) for i in range(2)]
        vec_ld, copied, waited, v_step = sem("vec_ld"), sem("idx_copied"), sem("waited"), sem("v_step")
        first, both, scaled, summed = sem("first_gated"), sem("both_gated"), sem("g2_applied"), sem("x_added")
        p_step, ready, normed, gained, x_ready = sem("p_step"), sem("factors_ready"), sem("normalised"), sem("gained"), sem("x_ready")
        landed, stored = [sem(f"y_landed{i}") for i in range(BUF)], sem("x_stored")
        with nc.Block() as block:
            @block.sync
            def _(sp):
                sp.dma_start(g2[:, :], g.mods[l, 0:1, 5 * D:6 * D].to_broadcast([P, D])).then_inc(vec_ld, 16)
                for j, n in enumerate(("ln2_g", "ln2_b")):
                    sp.dma_start(ln2[:, j, :], g.a[n][l:l + 1, :].to_broadcast([P, D])).then_inc(vec_ld, 16)
                for t in range(LT):
                    sp.wait_ge(x_ready, t + 1)
                    sp.dma_start(g.out[0, t * P:(t + 1) * P, :], g.x[:, t, :]).then_inc(stored, 16)
                sp.wait_ge(stored, 16 * LT)

            @block.gpsimd
            def _(pool):
                for t in range(BUF):
                    gather_experts(nc, pool, g, t, t, idx, ya, yb, landed, copied, waited)
                pool.wait_ge(vec_ld, 48)
                s = Steps(p_step)
                for t in range(LT + 1):
                    if t < LT:
                        m, r, k = mean[t % 2][:, :], rstd[t % 2][:, :], lambda c: g.k[:, c:c + 1]
                        if t >= 2:
                            pool.wait_ge(normed, t - 1)
                        pool.wait_ge(norm.var_ready, t + 1)
                        nc.gpsimd.tensor_tensor(r, norm.mv[:, 1:2], k(K_EPS), ALU.add).then_inc(s.sem, s.up())
                        nc.gpsimd.tensor_tensor(m, norm.mv[:, 0:1], k(K_NEG), ALU.mult).then_inc(s.sem, s.up())
                        pool.wait_ge(s.sem, s.at())
                        nc.gpsimd.tensor_tensor(r, r, k(K_NH), ALU.pow).then_inc(s.sem, s.up())
                        pool.wait_ge(s.sem, s.at())
                        nc.gpsimd.tensor_tensor(m, m, r, ALU.mult).then_inc(ready, 1)
                    if t:
                        y = ya[(t - 1) % BUF][:, :]
                        pool.wait_ge(gained, t)
                        nc.gpsimd.tensor_tensor(g.x[:, t - 1, :], y, ln2[:, 1, :], ALU.add).then_inc(x_ready, 1)
                        if t - 1 + BUF < LT:
                            pool.wait_ge(x_ready, t)
                            gather_experts(nc, pool, g, t - 1 + BUF, (t - 1) % BUF, idx, ya, yb, landed, copied, waited)

            @block.scalar
            def _(act):
                for t in range(LT + 1):
                    if t < LT:
                        y = ya[t % BUF][:, :]
                        act.wait_ge(landed[t % BUF], (t // BUF) * 32 + 32)
                        nc.scalar.activation(y, y, ACT.Copy, scale=g.gate[:, t, 0:1]).then_inc(first, 1)
                    if t:
                        y = ya[(t - 1) % BUF][:, :]
                        act.wait_ge(ready, t)
                        nc.scalar.activation(y, y, ACT.Identity, bias=mean[(t - 1) % 2][:, :], scale=rstd[(t - 1) % 2][:, :]).then_inc(normed, 1)

            @block.vector
            def _(v):
                s = Steps(v_step)
                for t in range(LT + 1):
                    if t < LT:
                        y, x = ya[t % BUF][:, :], g.x[:, t, :]
                        v.wait_ge(first, t + 1)
                        nc.vector.scalar_tensor_tensor(y, yb[t % BUF][:, :], g.gate[:, t, 1:2], y, ALU.mult, ALU.add).then_inc(both, 1)
                        v.wait_ge(both, t + 1)
                        if t == 0:
                            v.wait_ge(vec_ld, 48)
                        nc.vector.tensor_tensor(y, y, g2[:, :], ALU.mult).then_inc(scaled, 1)
                        v.wait_ge(scaled, t + 1)
                        nc.vector.scalar_tensor_tensor(y, x, ALPHA, y, ALU.mult, ALU.add).then_inc(summed, 1)
                        v.wait_ge(summed, t + 1)
                        if t:
                            v.wait_ge(ready, t)
                        rows_stats(nc, v, s, y, norm)
                    if t:
                        y = ya[(t - 1) % BUF][:, :]
                        v.wait_ge(normed, t)
                        nc.vector.tensor_tensor(y, y, ln2[:, 0, :], ALU.mult).then_inc(gained, 1)


def build(nc, a, out):
    g = Core()
    with ExitStack() as ctx:
        def sb(name, shape, dt=F32):
            return ctx.enter_context(nc.sbuf_tensor(name, shape, dt))

        g.a, g.out = a, out
        g.x = sb("x_res", [P, NT, D])
        g.k = sb("consts", [P, K_N])
        g.cols = sb("mod_cols", [P, DEPTH, 2, 2, KT])
        g.pos = sb("slot_of", [P, NT, 2], I32)
        g.gate = sb("gate_of", [P, NT, 2])
        g.ids = sb("token_ids", [P, NT], I32)
        g.logits = sb("logits", [P, NT, NR])
        g.mods = nc.dram_tensor("mods", [DEPTH, 2, 6 * D], F32).ap()
        g.h2 = nc.dram_tensor("h2_rows", [NT * P, D], F32).ap()
        g.y = nc.dram_tensor("expert_rows", [(NSLOTMAX + 1) * P, D], F32).ap()
        modulation(nc, g)
        for l in range(DEPTH):
            with ExitStack() as mix:
                def ms(name, shape, dt=F32):
                    return mix.enter_context(nc.sbuf_tensor(f"{name}{l}", shape, dt))
                m = Core()
                m.qT = ms("qT", [P, 2, NT * P])
                m.kT = ms("kT", [P, SEQ + 2 * P])
                m.kcT = ms("kcT", [P, CTX])
                m.v = ms("v_tok", [P, LT + 2 + CT, P])
                m.u = ms("u_tok", [P, NT, GW])
                m.sg = ms("sgu_v", [P, NT, GW])
                m.pT = ms("poolT", [P, 2, PW])
                m.a = ms("four_tok", [P, NT, GW])
                m.four = m.a[:, :, :].rearrange("p t c -> p (t c)").rearrange("p (h n) -> p h n", h=2)
                project(nc, g, m, l)
                transform(nc, g, m, l)
                attend(nc, g, m, l)
            route_and_experts(nc, g, l)
        finish(nc, g)
    return nc


_INS = ("x", "c", "ctx", "c_ctx", "w_ada", "b_ada", "w_in", "w_fourier", "attn_sink", "w_pool", "pool_scale", "w_sgu",
        "b_sgu", "w_out", "ln1_g", "ln1_b", "w_router_group", "w_router_expert", "w_exp_gate", "w_exp_up",
        "w_exp_down", "ln2_g", "ln2_b")


def kernel(**inputs):
    import concourse.bacc as bacc
    from concourse.bass_utils import run_bass_kernel_spmd

    nc = bacc.Bacc("TRN2", target_bir_lowering=False, num_devices=1)
    given = {n: np.asarray(inputs[n]) for n in _INS}
    given["w_sgu"] = given["w_sgu"].transpose(0, 3, 1, 2)
    w = given["w_in"]
    q = w[:, :, C_Q:C_K].reshape(DEPTH, D, 2, 2, HD).transpose(0, 1, 3, 2, 4).reshape(DEPTH, D, GW)
    given["w_in"] = np.concatenate([w[:, :, :C_Q], q, w[:, :, C_K:]], 2)
    given["b_sgu"] = given["b_sgu"].transpose(0, 2, 1)
    given["pool_scale"] = given["pool_scale"].reshape(DEPTH, 2, P).transpose(0, 2, 1)
    names = ("consts", "rope", "dft", "dft_ctx", "token_ids")
    given.update(zip(names, constant_tables()))
    arrays, aps = {}, {}
    for n, v in given.items():
        arrays["in_" + n] = np.ascontiguousarray(v)
        aps[n] = nc.dram_tensor("in_" + n, v.shape, mybir.dt.from_np(v.dtype), kind="ExternalInput").ap()
    out = nc.dram_tensor("out", (1, SEQ, D), F32, kind="ExternalOutput").ap()
    build(nc, aps, out)
    r = run_bass_kernel_spmd(nc, [arrays], core_ids=[0])
    return r.results[0]["out"]
```
